# Optimizing a Trainium2 kernel written in Bass

```python
import jax, jax.numpy as jnp
from jax import lax
import numpy as np

D_MODEL = 1024
BATCH = 1
SEQ = 1024
DEPTH = 2
DEC_BATCH = 8
DEC_SEQ = 4
PAST_LEN = 2048
PAGE_SIZE = 128

HEAD_DIM = 128
SB_HEADS = 12
BRANCH_WIDTH = 1536
MEM_HEADS = 4
MEM_WIDTH = 512
MIX_WIDTH = 2048
MEM_LEN = 256
POOL_WINDOWS = (2, 4, 8, 16)
POOL_GROUPS = 4
POOL_GROUP_WIDTH = 384
POOL_STATE_LEN = 15
POOL_IN_WIDTH = 4096
SB_IN_WIDTH = 7168
SB_BIAS_INIT = -7.0
Q_BLOCK = 128
RMS_EPS = 1e-6
N_POOL_LAYERS = (DEPTH + 1) // 2
N_SB_LAYERS = DEPTH // 2

kernel_name = "hybrid_pool_stickbreak_memory_decode_step"

def rms_norm(x, g):
    xf = x.astype(jnp.float32)
    y = xf * lax.rsqrt(jnp.mean(xf * xf, axis=-1, keepdims=True) + RMS_EPS)
    return (y * g.astype(jnp.float32)).astype(x.dtype)

def pool_mix(u_ext, pos, w_grp, scale):
    B, L, _ = u_ext.shape
    T = L - POOL_STATE_LEN
    uf = u_ext.astype(jnp.float32).reshape(B, L, POOL_GROUPS, POOL_GROUP_WIDTH)
    csum = jnp.concatenate([jnp.zeros_like(uf[:, :1]), jnp.cumsum(uf, axis=1)], axis=1)
    end = csum[:, POOL_STATE_LEN + 1:]
    means = []
    for g, w in enumerate(POOL_WINDOWS):
        start = csum[:, POOL_STATE_LEN + 1 - w:POOL_STATE_LEN + 1 - w + T, g]
        cnt = jnp.minimum(pos + 1, w).astype(jnp.float32)[None, :, None]
        means.append((end[:, :, g] - start) / cnt)
    pooled = jnp.stack(means, axis=2) - uf[:, POOL_STATE_LEN:]
    mixed = jnp.einsum('btgc,gcd->btgd', pooled, w_grp.astype(jnp.float32))
    return (mixed.reshape(B, T, BRANCH_WIDTH) * scale.astype(jnp.float32)).astype(u_ext.dtype)

def sb_block(q_blk, qpos_blk, k, v, kpos, bias):
    z = jnp.einsum('bqhd,bkhd->bhqk', q_blk.astype(jnp.float32), k.astype(jnp.float32)) * (HEAD_DIM ** -0.5)
    z = z + bias.astype(jnp.float32)[None, :, None, None]
    mask = kpos[None, :] < qpos_blk[:, None]
    log_beta = jax.nn.log_sigmoid(z)
    log_rem = jnp.where(mask, log_beta - z, 0.0)
    later = lax.cumsum(log_rem, axis=3, reverse=True) - log_rem
    a = jnp.where(mask, jnp.exp(log_beta + later), 0.0)
    return jnp.einsum('bhqk,bkhd->bqhd', a, v.astype(jnp.float32))

def stick_breaking(q, k, v, q_pos, k_pos, bias):
    B, Tq, H, Dh = q.shape
    blk = Q_BLOCK if Tq % Q_BLOCK == 0 else Tq
    nb = Tq // blk
    qb = q.reshape(B, nb, blk, H, Dh).transpose(1, 0, 2, 3, 4)
    pb = q_pos.reshape(nb, blk)
    out = lax.map(lambda a: sb_block(a[0], a[1], k, v, k_pos, bias), (qb, pb))
    return out.transpose(1, 0, 2, 3, 4).reshape(B, Tq, H * Dh).astype(q.dtype)

def mem_kv(mem, g_mem, w_mem_kv, g_k):
    B, M, _ = mem.shape
    kv = rms_norm(mem, g_mem) @ w_mem_kv
    k = rms_norm(kv[..., :MEM_WIDTH].reshape(B, M, MEM_HEADS, HEAD_DIM), g_k)
    v = kv[..., MEM_WIDTH:].reshape(B, M, MEM_HEADS, HEAD_DIM)
    return k, v

def merge_out(branch, gate, mq, mgate, mk, mv, g_q, w_out):
    B, T, _ = mq.shape
    q = rms_norm(mq.reshape(B, T, MEM_HEADS, HEAD_DIM), g_q)
    s = jnp.einsum('bqhd,bmhd->bhqm', q.astype(jnp.float32), mk.astype(jnp.float32)) * (HEAD_DIM ** -0.5)
    p = jax.nn.softmax(s, axis=-1)
    mo = jnp.einsum('bhqm,bmhd->bqhd', p, mv.astype(jnp.float32)).reshape(B, T, MEM_WIDTH).astype(mq.dtype)
    y = jnp.concatenate([branch * jax.nn.silu(gate), mo * jax.nn.silu(mgate)], axis=-1)
    return y @ w_out

def setup_inputs(seed: int = 0) -> dict:
    key = jax.random.key(seed)
    ks = jax.random.split(key, 21)
    f32 = jnp.float32
    n_pages = PAST_LEN // PAGE_SIZE
    n_used = DEC_BATCH * n_pages
    n_phys = n_used + n_used // 4

    def nrm(k, shape, scale=1.0):
        return jax.random.normal(k, shape, f32) * scale

    page_table = jax.random.permutation(ks[7], n_phys)[:n_used].reshape(DEC_BATCH, n_pages).astype(jnp.int32)
    return {
        "x_prompt": nrm(ks[0], (BATCH, SEQ, D_MODEL)),
        "x_sample": nrm(ks[1], (DEC_BATCH, DEC_SEQ, D_MODEL)),
        "cache_mem_k": nrm(ks[2], (DEPTH, DEC_BATCH, MEM_LEN, MEM_HEADS, HEAD_DIM)),
        "cache_mem_v": nrm(ks[3], (DEPTH, DEC_BATCH, MEM_LEN, MEM_HEADS, HEAD_DIM)),
        "state_pool": nrm(ks[4], (N_POOL_LAYERS, DEC_BATCH, POOL_STATE_LEN, BRANCH_WIDTH)),
        "cache_sb_k": nrm(ks[5], (N_SB_LAYERS, n_phys, PAGE_SIZE, SB_HEADS, HEAD_DIM)),
        "cache_sb_v": nrm(ks[6], (N_SB_LAYERS, n_phys, PAGE_SIZE, SB_HEADS, HEAD_DIM)),
        "page_table": page_table,
        "mem_prompt": nrm(ks[8], (BATCH, MEM_LEN, D_MODEL)),
        "norm_g": 1.0 + nrm(ks[9], (DEPTH, D_MODEL), 0.05),
        "w_in_pool": nrm(ks[10], (N_POOL_LAYERS, D_MODEL, POOL_IN_WIDTH), D_MODEL ** -0.5),
        "w_pool_grp": nrm(ks[11], (N_POOL_LAYERS, POOL_GROUPS, POOL_GROUP_WIDTH, POOL_GROUP_WIDTH), POOL_GROUP_WIDTH ** -0.5),
        "pool_scale": 1.0 + nrm(ks[12], (N_POOL_LAYERS, BRANCH_WIDTH), 0.05),
        "w_in_sb": nrm(ks[13], (N_SB_LAYERS, D_MODEL, SB_IN_WIDTH), D_MODEL ** -0.5),
        "sb_bias": SB_BIAS_INIT + nrm(ks[19], (N_SB_LAYERS, SB_HEADS), 0.3),
        "mem_norm_g": 1.0 + nrm(ks[14], (DEPTH, D_MODEL), 0.05),
        "w_mem_kv": nrm(ks[15], (DEPTH, D_MODEL, 2 * MEM_WIDTH), D_MODEL ** -0.5),
        "mem_q_g": 1.0 + nrm(ks[16], (DEPTH, HEAD_DIM), 0.05),
        "mem_k_g": 1.0 + nrm(ks[17], (DEPTH, HEAD_DIM), 0.05),
        "w_out": nrm(ks[18], (DEPTH, MIX_WIDTH, D_MODEL), MIX_WIDTH ** -0.5),
    }

def reference(x_prompt, x_sample, cache_mem_k, cache_mem_v, state_pool, cache_sb_k, cache_sb_v, page_table,
              mem_prompt, norm_g, w_in_pool, w_pool_grp, pool_scale, w_in_sb, sb_bias, mem_norm_g, w_mem_kv,
              mem_q_g, mem_k_g, w_out):
    B, T = x_prompt.shape[0], x_prompt.shape[1]
    Bd, Td = x_sample.shape[0], x_sample.shape[1]
    n_pages = page_table.shape[1]
    past = n_pages * cache_sb_k.shape[2]
    pos_p = jnp.arange(T, dtype=jnp.int32)
    pos_s = past + jnp.arange(Td, dtype=jnp.int32)
    kpos_s = jnp.arange(past + Td, dtype=jnp.int32)
    bw, mw = BRANCH_WIDTH, MEM_WIDTH

    xp, xs = x_prompt, x_sample
    mk_out, mv_out = [], []
    pool_p_out, pool_s_out = [], []
    sbk_p_out, sbv_p_out, sbk_s_out, sbv_s_out = [], [], [], []
    for i in range(DEPTH):
        j = i // 2
        hp = rms_norm(xp, norm_g[i])
        hs = rms_norm(xs, norm_g[i])
        mk_p, mv_p = mem_kv(mem_prompt, mem_norm_g[i], w_mem_kv[i], mem_k_g[i])
        mk_out.append(mk_p)
        mv_out.append(mv_p)
        if i % 2 == 0:
            zp = hp @ w_in_pool[j]
            zs = hs @ w_in_pool[j]
            u_p, gate_p, mq_p, mg_p = zp[..., :bw], zp[..., bw:2 * bw], zp[..., 2 * bw:2 * bw + mw], zp[..., 2 * bw + mw:]
            u_s, gate_s, mq_s, mg_s = zs[..., :bw], zs[..., bw:2 * bw], zs[..., 2 * bw:2 * bw + mw], zs[..., 2 * bw + mw:]
            u_p_ext = jnp.concatenate([jnp.zeros((B, POOL_STATE_LEN, bw), u_p.dtype), u_p], axis=1)
            u_s_ext = jnp.concatenate([state_pool[j].astype(u_s.dtype), u_s], axis=1)
            br_p = pool_mix(u_p_ext, pos_p, w_pool_grp[j], pool_scale[j])
            br_s = pool_mix(u_s_ext, pos_s, w_pool_grp[j], pool_scale[j])
            pool_p_out.append(u_p_ext[:, -POOL_STATE_LEN:])
            pool_s_out.append(u_s_ext[:, -POOL_STATE_LEN:])
        else:
            zp = hp @ w_in_sb[j]
            zs = hs @ w_in_sb[j]
            q_p = zp[..., :bw].reshape(B, T, SB_HEADS, HEAD_DIM)
            k_p = zp[..., bw:2 * bw].reshape(B, T, SB_HEADS, HEAD_DIM)
            v_p = zp[..., 2 * bw:3 * bw].reshape(B, T, SB_HEADS, HEAD_DIM)
            gate_p, mq_p, mg_p = zp[..., 3 * bw:4 * bw], zp[..., 4 * bw:4 * bw + mw], zp[..., 4 * bw + mw:]
            q_s = zs[..., :bw].reshape(Bd, Td, SB_HEADS, HEAD_DIM)
            k_s = zs[..., bw:2 * bw].reshape(Bd, Td, SB_HEADS, HEAD_DIM)
            v_s = zs[..., 2 * bw:3 * bw].reshape(Bd, Td, SB_HEADS, HEAD_DIM)
            gate_s, mq_s, mg_s = zs[..., 3 * bw:4 * bw], zs[..., 4 * bw:4 * bw + mw], zs[..., 4 * bw + mw:]
            br_p = stick_breaking(q_p, k_p, v_p, pos_p, pos_p, sb_bias[j])
            k_past = cache_sb_k[j][page_table].reshape(Bd, past, SB_HEADS, HEAD_DIM).astype(k_s.dtype)
            v_past = cache_sb_v[j][page_table].reshape(Bd, past, SB_HEADS, HEAD_DIM).astype(v_s.dtype)
            k_all = jnp.concatenate([k_past, k_s], axis=1)
            v_all = jnp.concatenate([v_past, v_s], axis=1)
            br_s = stick_breaking(q_s, k_all, v_all, pos_s, kpos_s, sb_bias[j])
            sbk_p_out.append(k_p)
            sbv_p_out.append(v_p)
            sbk_s_out.append(k_s)
            sbv_s_out.append(v_s)
        xp = xp + merge_out(br_p, gate_p, mq_p, mg_p, mk_p, mv_p, mem_q_g[i], w_out[i])
        xs = xs + merge_out(br_s, gate_s, mq_s, mg_s, cache_mem_k[i], cache_mem_v[i], mem_q_g[i], w_out[i])

    new_mem_k_prompt = jnp.stack(mk_out)
    new_mem_v_prompt = jnp.stack(mv_out)
    new_pool_state_prompt = jnp.stack(pool_p_out)
    new_pool_state_sample = jnp.stack(pool_s_out)
    new_sb_k_prompt = jnp.stack(sbk_p_out)
    new_sb_v_prompt = jnp.stack(sbv_p_out)
    new_sb_k_sample = jnp.stack(sbk_s_out)
    new_sb_v_sample = jnp.stack(sbv_s_out)
    return (xp, xs, new_mem_k_prompt, new_mem_v_prompt, new_pool_state_prompt, new_pool_state_sample,
            new_sb_k_prompt, new_sb_v_prompt, new_sb_k_sample, new_sb_v_sample)


_drawn_inputs = setup_inputs


def setup_inputs(seed=0):
    import zlib

    import numpy as np

    out = dict(_drawn_inputs(seed))
    spreads = {}
    factors = {'cache_sb_k': 3.065, 'pool_scale': 2.769, 'sb_bias': 8.0, 'mem_q_g': 8.0}
    for name, (base, spread) in spreads.items():
        noise = np.random.default_rng([zlib.crc32(name.encode()), seed]).standard_normal(out[name].shape)
        drawn = base * np.exp(spread * noise) if base else spread * noise
        out[name] = __import__('jax').numpy.asarray(drawn.astype(out[name].dtype))
    for name, factor in factors.items():
        out[name] = (out[name] * factor).astype(out[name].dtype)
    return out
```

```python
from contextlib import ExitStack

import concourse.bass as bass
from concourse import mybir

F32 = mybir.dt.float32
F32R = mybir.dt.float32r
I32 = mybir.dt.int32
ALU = mybir.AluOpType
ACT = mybir.ActivationFunctionType
AX_X = mybir.AxisListType.X

P = 128
D = 1024
KD = D // P
SEQ = 1024
NB_S, T_S = 8, 4
SAMPLES = NB_S * T_S
T = SEQ + SAMPLES
NT = 3
TT = T // NT
TILES = SEQ // P
LAST = T - P
HEADS, HD = 12, 128
BW = HEADS * HD
MH = 4
MW = MH * HD
MEM = 256
MJ = MEM // P
GROUPS, GB = 4, 3
GW = GB * P
WINDOWS = (2, 4, 8, 16)
HIST = 15
PAGE = 128
PAGES = 16
EPS = 1e-6
SCALE = float(HD) ** -0.5
NEG = -1e30
KU = GW


class Kit:

    def __init__(self, nc, ctx, tag):
        self.nc, self.ctx, self.tag, self.sems = nc, ctx, tag, []
        ctx.callback(self.release)

    def sb(self, name, shape, dt=F32):
        return self.ctx.enter_context(self.nc.sbuf_tensor(self.tag + name, shape, dt))

    def ps(self, name, n=1):
        banks = [self.ctx.enter_context(self.nc.psum_tensor(f"{self.tag}{name}{i}", [P, 512], F32)) for i in range(n)]
        return banks if n > 1 else banks[0]

    def sem(self, name):
        handle = self.nc.alloc_semaphore(name=self.tag + name)
        self.sems.append(handle)
        return handle

    def release(self):
        if self.sems:
            self.nc.clear_and_free_semaphores(self.sems)
            self.nc.all_engine_barrier()


def product3(pe, out, stat_hi, stat_lo, mov_hi, mov_lo, first, last):
    pe.matmul(out, stat_hi, mov_hi, start=first, stop=False)
    pe.matmul(out, stat_hi, mov_lo, start=False, stop=False)
    return pe.matmul(out, stat_lo, mov_hi, start=False, stop=last)


def setup_phase(nc, c, A):
    with ExitStack() as ctx:
        k = Kit(nc, ctx, "s_")
        rows = k.sb("vector_rows", [P, P])
        row0 = k.sb("row0", [1, 2 * HD + HEADS])
        pos = k.sb("pos", [P, 16], I32)
        rec = k.sb("rec", [P, 16])
        posf = k.sb("posf", [P, 16])
        bank = k.ps("bank", 2)
        loaded, made, turned, kept, steps = (k.sem(n) for n in ("loaded", "made", "turned", "kept", "steps"))
        NV = 46
        with nc.Block() as block:
            @block.sync
            def _(sp):
                sp.dma_start(rows[0:16, :], A["norm_g"].rearrange("l (k p) -> (l k) p", p=P)).then_inc(loaded, 16)
                sp.dma_start(rows[16:32, :], A["mem_norm_g"].rearrange("l (k p) -> (l k) p", p=P)).then_inc(loaded, 16)
                sp.dma_start(rows[32:44, :], A["pool_scale"].rearrange("l (k p) -> (l k) p", p=P)).then_inc(loaded, 16)
                sp.dma_start(rows[44:46, :], A["mem_q_g"]).then_inc(loaded, 16)
                sp.dma_start(row0[:, 0:2 * HD], A["mem_k_g"].rearrange("(o l) d -> o (l d)", o=1)).then_inc(loaded, 16)
                sp.dma_start(row0[:, 2 * HD:], A["sb_bias"]).then_inc(loaded, 16)

            @block.gpsimd
            def _(gp):
                gp.memset(c["ident"][:, :], 0.0).then_inc(steps, 1)
                gp.memset(c["ones"][:, :], 1.0).then_inc(steps, 1)
                gp.iota(pos[:, :], pattern=[[1, 16]], base=1, channel_multiplier=0).then_inc(steps, 1)
                gp.memset(c["neg"][:, :], 0.0).then_inc(steps, 1)
                gp.wait_ge(steps, 4)
                gp.affine_select(out=c["ident"][:, :], in_=c["ident"][:, :], compare_op=ALU.not_equal, fill=1.0,
                                 base=0, pattern=[[-1, P]], channel_multiplier=1).then_inc(made, 1)
                gp.affine_select(out=c["suffix"][:, :], in_=c["ones"][:, :], compare_op=ALU.is_ge, fill=0.0,
                                 base=0, pattern=[[-1, P]], channel_multiplier=1).then_inc(made, 1)
                gp.affine_select(out=c["before"][:, :], in_=c["ones"][:, :], compare_op=ALU.is_gt, fill=0.0,
                                 base=0, pattern=[[1, P]], channel_multiplier=-1).then_inc(made, 1)
                gp.affine_select(out=c["neg"][:, :], in_=c["neg"][:, :], compare_op=ALU.is_gt, fill=NEG,
                                 base=0, pattern=[[1, P]], channel_multiplier=-1).then_inc(made, 1)
                keep = c["keep_new"][:, :].rearrange("p (b t) -> p b t", t=T_S)
                gp.affine_select(out=keep, in_=c["ones"][0:SAMPLES, 0:SAMPLES].rearrange("p (b t) -> p b t", t=T_S),
                                 compare_op=ALU.is_ge, fill=0.0, base=0, pattern=[[-T_S, NB_S], [0, T_S]],
                                 channel_multiplier=1).then_inc(steps, 1)
                gp.wait_ge(steps, 5)
                gp.affine_select(out=keep, in_=keep, compare_op=ALU.is_gt, fill=0.0, base=0,
                                 pattern=[[T_S, NB_S], [1, T_S]], channel_multiplier=-1).then_inc(made, 1)

            @block.tensor
            def _(pe):
                pe.wait_ge(made, 5)
                pe.wait_ge(loaded, 96)
                pe.transpose(bank[0][:, 0:NV], rows[0:NV, :], c["ident"][0:NV, 0:NV])
                pe.matmul(bank[1][:, 0:2 * HD + HEADS], c["ones"][0:1, :], row0[:, :], start=True,
                          stop=True).then_inc(turned, 1)

            @block.vector
            def _(dve):
                dve.wait_ge(steps, 3)
                dve.tensor_copy(posf[:, :], pos[:, :]).then_inc(kept, 1)
                dve.wait_ge(kept, 1)
                dve.reciprocal(rec[:, :], posf[:, :]).then_inc(kept, 1)
                dve.wait_ge(kept, 2)
                for g, w in enumerate(WINDOWS):
                    dve.tensor_scalar(c["short"][:, g, :], rec[:, :], float(w), 1.0, ALU.mult, ALU.max).then_inc(kept, 1)
                dve.wait_ge(turned, 1)
                dve.tensor_copy(c["vec"][:, :], bank[0][:, 0:NV]).then_inc(kept, 1)
                dve.tensor_copy(c["rowb"][:, :], bank[1][:, 0:2 * HD + HEADS]).then_inc(kept, 1)
                dve.wait_ge(made, 5)
                dve.tensor_scalar(c["neg_new"][:, :], c["keep_new"][:, :], 1.0, -NEG, ALU.subtract,
                                  ALU.mult).then_inc(kept, 1)
                dve.wait_ge(made, 4)
                dve.tensor_scalar(c["keep"][:, :], c["neg"][:, :], 1.0 / -NEG, 1.0, ALU.mult, ALU.add).then_inc(kept, 1)


def norm_phase(nc, c, hT_hi, hT_lo, source, gain):
    with ExitStack() as ctx:
        k = Kit(nc, ctx, f"n{gain}_")
        x = k.sb("x", [P, 2, D])
        xn = k.sb("xn", [P, 2, D])
        junk = k.sb("junk", [P, D])
        ss = k.sb("ss", [P, 4 * (TILES + 1)])
        bank = k.ps("bank", 4)
        loaded = [k.sem(f"loaded{i}") for i in range(2)]
        squared, mean, root, inv, normed, turned, hi, lo = (
            k.sem(n) for n in ("squared", "mean", "root", "inv", "normed", "turned", "hi", "lo"))
        N = TILES + 1
        col = lambda what, t: ss[:, what * N + t:what * N + t + 1]
        tok = lambda t: t * P if t < TILES else LAST
        with nc.Block() as block:
            @block.sync
            def _(sp):
                for t in range(N):
                    if t >= 2:
                        sp.wait_ge(normed, t - 1)
                    pieces = source(t)
                    for r0, r1, src in pieces:
                        sp.dma_start(x[r0:r1, t % 2, :], src).then_inc(loaded[t % 2], 32 // len(pieces))

            @block.scalar
            def _(act):
                def evacuate(t):
                    for kk in range(KD):
                        if kk % 4 == 0:
                            act.wait_ge(turned, 2 * t + kk // 4 + 1)
                        if t == N - 1 and kk == 0:
                            act.wait_ge(lo, KD * t)
                        act.activation(hT_hi[:, kk, tok(t):tok(t) + P], bank[2 * (t % 2) + kk // 4][:, (kk % 4) * P:(kk % 4 + 1) * P],
                                       ACT.Identity,
                                       scale=c["vec"][:, gain + kk:gain + kk + 1]).then_inc(hi, 1)
                for t in range(N):
                    act.wait_ge(loaded[t % 2], 32 * (t // 2 + 1))
                    if t >= 1:
                        act.wait_ge(squared, t)
                    act.activation(junk[:, :], x[:, t % 2, :], ACT.Square, accum_out=col(0, t)).then_inc(squared, 1)
                    act.wait_ge(mean, t + 1)
                    act.activation(col(2, t), col(1, t), ACT.Sqrt).then_inc(root, 1)
                    if t >= 1:
                        evacuate(t - 1)
                evacuate(N - 1)

            @block.vector
            def _(dve):
                def rest(t):
                    for kk in range(KD):
                        dve.wait_ge(hi, KD * t + 4 * (kk // 4) + 4)
                        out = hT_lo[:, kk, tok(t):tok(t) + P]
                        dve.scalar_tensor_tensor(
                            out=out, in0=bank[2 * (t % 2) + kk // 4][:, (kk % 4) * P:(kk % 4 + 1) * P],
                            scalar=c["vec"][:, gain + kk:gain + kk + 1],
                            in1=hT_hi[:, kk, tok(t):tok(t) + P].bitcast(F32), op0=ALU.mult, op1=ALU.subtract).then_inc(lo, 1)
                for t in range(N):
                    dve.wait_ge(squared, t + 1)
                    dve.tensor_scalar(col(1, t), col(0, t), 1.0 / D, EPS, ALU.mult, ALU.add).then_inc(mean, 1)
                    dve.wait_ge(root, t + 1)
                    dve.reciprocal(col(3, t), col(2, t)).then_inc(inv, 1)
                    dve.wait_ge(inv, t + 1)
                    if t >= 2:
                        dve.wait_ge(turned, 2 * t - 2)
                    dve.tensor_scalar(xn[:, t % 2, :], x[:, t % 2, :], col(3, t), None, ALU.mult).then_inc(normed, 1)
                    if t >= 1:
                        rest(t - 1)
                rest(N - 1)

            @block.tensor
            def _(pe):
                for t in range(N):
                    pe.wait_ge(normed, t + 1)
                    if t >= 2:
                        pe.wait_ge(lo, KD * (t - 1))
                    for kk in range(KD):
                        ins = pe.transpose(bank[2 * (t % 2) + kk // 4][:, (kk % 4) * P:(kk % 4 + 1) * P],
                                           xn[:, t % 2, kk * P:(kk + 1) * P], c["ident"][:, :])
                        if kk % 4 == 3:
                            ins.then_inc(turned, 1)


def memory_kv_phase(nc, c, A, O, i):
    with ExitStack() as ctx:
        k = Kit(nc, ctx, f"m{i}_")
        x = k.sb("x", [P, MJ, D])
        xn = k.sb("xn", [P, MJ, D])
        xT = k.sb("xT", [P, KD, MEM])
        junk = k.sb("junk", [P, D])
        st = k.sb("st", [P, 4, 8])
        mT_hi = k.sb("mT_hi", [P, KD, MEM], F32R)
        mT_lo = k.sb("mT_lo", [P, KD, MEM], F32R)
        w = k.sb("w", [P, KD, MW])
        w_hi = k.sb("w_hi", [P, KD, MW], F32R)
        w_lo = k.sb("w_lo", [P, KD, MW], F32R)
        kn = k.sb("kn", [P, 2, MW])
        ks = k.sb("ks", [P, 4, 2 * 2 * MH])
        bank = k.ps("bank", 4)
        kb = k.ps("kb", 4)
        names = ("loaded squared mean root inv normed turned kept weights whi wlo thi tlo made ksq kmean kroot kinv "
                 "kout kturned kstored vout").split()
        s = {n: k.sem(n) for n in names}
        with nc.Block() as block:
            @block.sync
            def _(sp):
                for j in range(MJ):
                    sp.dma_start(x[:, j, :], A["mem_prompt"][0, j * P:(j + 1) * P, :]).then_inc(s["loaded"], 16)
                for n in range(2):
                    if n:
                        sp.wait_ge(s["wlo"], n)
                    v = n
                    sp.dma_start(w[:, :, :], A["w_mem_kv"][i, :, v * MW:(v + 1) * MW].rearrange(
                        "(k p) n -> p k n", p=P)).then_inc(s["weights"], 16)
                    if n % 2 == 1:
                        for j in range(MJ):
                            sp.wait_ge(s["kout"], j + 1)
                            sp.dma_start(O["mem_k"][i, 0, j * P:(j + 1) * P].rearrange("p h d -> p (h d)"),
                                         kn[:, j, :]).then_inc(s["kstored"], 16)
                        for j in range(MJ):
                            sp.wait_ge(s["vout"], j + 1)
                            sp.dma_start(O["mem_v"][i, 0, j * P:(j + 1) * P].rearrange("p h d -> p (h d)"),
                                         c["mv"][:, j, :]).then_inc(s["kstored"], 16)
                sp.wait_ge(s["kstored"], 16 * 4)

            @block.scalar
            def _(act):
                act.wait_ge(s["loaded"], 16 * MJ)
                for j in range(MJ):
                    if j:
                        act.wait_ge(s["squared"], j)
                    act.activation(junk[:, :], x[:, j, :], ACT.Square, accum_out=st[:, 0, j:j + 1]).then_inc(s["squared"], 1)
                act.wait_ge(s["mean"], 1)
                act.activation(st[:, 2, 0:MJ], st[:, 1, 0:MJ], ACT.Sqrt).then_inc(s["root"], 1)
                for n in range(2):
                    act.wait_ge(s["weights"], 16 * (n + 1))
                    if n:
                        act.wait_ge(s["made"], 2 * n)
                    act.activation(w_hi[:, :, :], w[:, :, :], ACT.Copy).then_inc(s["whi"], 1)
                    if n % 2 == 0:
                        act.wait_ge(s["kept"], 4)
                        for kk in range(KD):
                            g = 16 + 8 * i + kk
                            act.activation(mT_hi[:, kk, :], xT[:, kk, :], ACT.Identity,
                                           scale=c["vec"][:, g:g + 1]).then_inc(s["thi"], 1)
                        for j in range(MJ):
                            act.wait_ge(s["made"], 2 * n + j + 1)
                            for h in range(MH):
                                if (j, h) != (0, 0):
                                    act.wait_ge(s["ksq"], 4 * j + h)
                                act.activation(junk[:, 0:HD], bank[2 * (n % 2) + j][:, h * HD:(h + 1) * HD], ACT.Square,
                                               accum_out=ks[:, 0, 4 * j + h:4 * j + h + 1]).then_inc(s["ksq"], 1)
                            act.wait_ge(s["kmean"], j + 1)
                            a = slice(4 * j, 4 * j + 4)
                            act.activation(ks[:, 2, a], ks[:, 1, a], ACT.Sqrt).then_inc(s["kroot"], 1)
                    else:
                        for j in range(MJ):
                            act.wait_ge(s["made"], 2 * n + j + 1)
                            act.activation(c["mv"][:, j, :], bank[2 * (n % 2) + j][:, :], ACT.Copy).then_inc(s["vout"], 1)

            @block.vector
            def _(dve):
                dve.wait_ge(s["squared"], MJ)
                dve.tensor_scalar(st[:, 1, 0:MJ], st[:, 0, 0:MJ], 1.0 / D, EPS, ALU.mult, ALU.add).then_inc(s["mean"], 1)
                dve.wait_ge(s["root"], 1)
                dve.reciprocal(st[:, 3, 0:MJ], st[:, 2, 0:MJ]).then_inc(s["inv"], 1)
                dve.wait_ge(s["inv"], 1)
                for j in range(MJ):
                    dve.tensor_scalar(xn[:, j, :], x[:, j, :], st[:, 3, j:j + 1], None, ALU.mult).then_inc(s["normed"], 1)
                for q in range(4):
                    dve.wait_ge(s["turned"], q + 1)
                    dve.tensor_copy(xT[:, 2 * q:2 * q + 2, :], kb[q][:, :].rearrange("p (k m) -> p k m", k=2)).then_inc(s["kept"], 1)
                for n in range(2):
                    dve.wait_ge(s["whi"], n + 1)
                    dve.tensor_tensor(w_lo[:, :, :], w[:, :, :], w_hi[:, :, :].bitcast(F32), ALU.subtract).then_inc(s["wlo"], 1)
                    if n % 2 == 0:
                        if n == 0:
                            dve.wait_ge(s["kept"], 4)
                        for kk in range(KD):
                            dve.wait_ge(s["thi"], kk + 1)
                            g = 16 + 8 * i + kk
                            dve.scalar_tensor_tensor(out=mT_lo[:, kk, :], in0=xT[:, kk, :], scalar=c["vec"][:, g:g + 1],
                                                     in1=mT_hi[:, kk, :].bitcast(F32), op0=ALU.mult,
                                                     op1=ALU.subtract).then_inc(s["tlo"], 1)
                        for j in range(MJ):
                            a = slice(4 * j, 4 * j + 4)
                            dve.wait_ge(s["ksq"], 4 * j + 4)
                            dve.tensor_scalar(ks[:, 1, a], ks[:, 0, a], 1.0 / HD, EPS, ALU.mult, ALU.add).then_inc(s["kmean"], 1)
                            dve.wait_ge(s["kroot"], j + 1)
                            dve.reciprocal(ks[:, 3, a], ks[:, 2, a]).then_inc(s["kinv"], 1)
                            dve.wait_ge(s["kinv"], j + 1)
                            for h in range(MH):
                                ins = dve.scalar_tensor_tensor(
                                    out=kn[:, j, h * HD:(h + 1) * HD], in0=bank[2 * (n % 2) + j][:, h * HD:(h + 1) * HD],
                                    scalar=ks[:, 3, 4 * j + h:4 * j + h + 1],
                                    in1=c["rowb"][:, i * HD:(i + 1) * HD], op0=ALU.mult, op1=ALU.mult)
                            ins.then_inc(s["kout"], 1)
                        for q in range(2):
                            dve.wait_ge(s["kturned"], q + 1)
                            dve.tensor_scalar(c["mkT"][:, 2 * q:2 * q + 2, :], kb[q][:, :].rearrange("p (h m) -> p h m", h=2),
                                              c["vec"][:, 44 + i:45 + i], None, ALU.mult).then_inc(s["kept"], 1)

            @block.tensor
            def _(pe):
                pe.wait_ge(s["normed"], MJ)
                for q in range(4):
                    for kk in range(2):
                        for j in range(MJ):
                            ins = pe.transpose(kb[q][:, kk * MEM + j * P:kk * MEM + (j + 1) * P],
                                               xn[:, j, (2 * q + kk) * P:(2 * q + kk + 1) * P], c["ident"][:, :])
                    ins.then_inc(s["turned"], 1)
                for n in range(2):
                    pe.wait_ge(s["wlo"], n + 1)
                    pe.wait_ge(s["tlo"], KD)
                    for j in range(MJ):
                        for kk in range(KD):
                            ins = product3(pe, bank[2 * (n % 2) + j][:, :], mT_hi[:, kk, j * P:(j + 1) * P],
                                           mT_lo[:, kk, j * P:(j + 1) * P], w_hi[:, kk, :], w_lo[:, kk, :],
                                           kk == 0, kk == KD - 1)
                        ins.then_inc(s["made"], 1)
                    if n % 2 == 0:
                        pe.wait_ge(s["kept"], 4)
                        pe.wait_ge(s["kout"], 2)
                        for q in range(2):
                            for hh in range(2):
                                for j in range(MJ):
                                    h = 2 * q + hh
                                    ins = pe.transpose(kb[q][:, hh * MEM + j * P:hh * MEM + (j + 1) * P],
                                                       kn[:, j, h * HD:(h + 1) * HD], c["ident"][:, :])
                            ins.then_inc(s["kturned"], 1)


def pool_phase(nc, c, A, O, S, hT_hi, hT_lo):
    with ExitStack() as ctx:
        k = Kit(nc, ctx, "p_")
        EXT = HIST + SEQ
        SX = HIST + T_S
        w = [k.sb(f"w{i}", [P, KD, KU]) for i in range(2)]
        w_hi = [k.sb(f"w_hi{i}", [P, KD, KU], F32R) for i in range(2)]
        w_lo = [k.sb(f"w_lo{i}", [P, KD, KU], F32R) for i in range(2)]
        wg = k.sb("wg", [P, GB, GW])
        up = k.sb("up", [P, GB, EXT])
        us = k.sb("us", [P, GB, NB_S, SX])
        un = k.sb("un", [P, GB, SAMPLES])
        sums = [k.sb(f"sum{i}", [P, EXT]) for i in range(2)]
        ssum = [k.sb(f"ssum{i}", [P, NB_S, SX]) for i in range(2)]
        gate = k.sb("gate", [P, GB, T])
        state = k.sb("state", [NB_S * HIST, BW])
        tail = k.sb("tail", [SAMPLES, 2, GW])
        bank = k.ps("bank", 6)
        aux = k.ps("aux", 2)
        wl = [k.sem(f"wl{i}") for i in range(2)]
        names = ("whi wlo wgl uready uevac stl zeroed sturned pooled mixed mready sums tailt tailc stored "
                 "ystored carried").split()
        s = {n: k.sem(n) for n in names}
        pooledT = k.sb("pooledT", [P, GB, T])
        w_src = A["w_in_pool"][0]
        offset = lambda j: (j // 2) * GW + (j % 2) * BW
        unit = lambda n: slice(n * TT, (n + 1) * TT)

        def finish_group(sp, g):
            sp.wait_ge(s["tailc"], 2 * g + 2)
            sp.dma_start(O["pool_p"][0, 0, :, g * GW:(g + 1) * GW], tail[0:HIST, 0, :]).then_inc(s["stored"], 16)
            sp.dma_start(O["pool_s"][0, :, HIST - T_S:HIST, g * GW:(g + 1) * GW], tail[:, 1, :]).then_inc(s["stored"], 16)
            for m in range(GB):
                sp.wait_ge(s["mixed"], 9 + 9 * g + 3 * m + 3)
                sp.dma_start(S["yT"][g * GB + m], gate[:, m, :]).then_inc(s["ystored"], 16)

        with nc.Block() as block:
            @block.sync
            def _(sp):
                sp.dma_start(state[:, :], A["state_pool"][0].rearrange("b s n -> (b s) n")).then_inc(s["stl"], 16)
                sp.dma_start(O["pool_s"][0, :, 0:HIST - T_S, :], A["state_pool"][0, :, T_S:HIST, :]).then_inc(s["carried"], 16)

                def load_group(g):
                    if g:
                        sp.wait_ge(s["mready"], 9 * g)
                    sp.dma_start(wg[:, :, :], A["w_pool_grp"][0, g].rearrange(
                        "(k p) n -> p k n", p=P)).then_inc(s["wgl"], 16)
                for j in range(2 * GROUPS):
                    if j >= 2:
                        sp.wait_ge(s["wlo"], j - 1)
                    sp.dma_start(w[j % 2][:, :, :], w_src[:, offset(j):offset(j) + KU].rearrange(
                        "(k p) n -> p k n", p=P)).then_inc(wl[j % 2], 16)
                    if j == 0:
                        load_group(0)
                    if j >= 3 and j % 2 == 1:
                        finish_group(sp, (j - 3) // 2)
                        load_group((j - 1) // 2)
                finish_group(sp, GROUPS - 1)
                sp.wait_ge(s["ystored"], 16 * GB * GROUPS)
                sp.wait_ge(s["stored"], 32 * GROUPS)
                sp.wait_ge(s["carried"], 16)

            @block.scalar
            def _(act):
                def part(j):
                    act.wait_ge(wl[j % 2], 16 * (j // 2 + 1))
                    if j >= 2:
                        act.wait_ge(s["uready"], 9 * (j - 1))
                    act.activation(w_hi[j % 2][:, :, :], w[j % 2][:, :, :], ACT.Copy).then_inc(s["whi"], 1)
                part(0)
                part(1)
                act.wait_ge(s["zeroed"], 1)
                for g in range(GROUPS):
                    if g:
                        act.wait_ge(s["pooled"], g)
                        act.wait_ge(s["tailt"], 2 * g)
                    for m in range(GB):
                        for n in range(NT):
                            act.wait_ge(s["uready"], 18 * g + 3 * m + n + 1)
                            b = bank[((m % 2) * 3) + n]
                            cols = min((n + 1) * TT, SEQ) - n * TT
                            ins = act.activation(up[:, m, HIST + n * TT:HIST + n * TT + cols], b[:, 0:cols], ACT.Copy)
                            if n == NT - 1:
                                act.activation(un[:, m, :], b[:, cols:TT], ACT.Copy)
                                ins = act.activation(us[:, m, :, HIST:SX], b[:, cols:TT].rearrange(
                                    "p (b t) -> p b t", t=T_S), ACT.Copy)
                            ins.then_inc(s["uevac"], 1)
                    if g < GROUPS - 1:
                        part(2 * g + 2)
                    if g:
                        act.wait_ge(s["ystored"], 16 * GB * g)
                    for m in range(GB):
                        for n in range(NT):
                            act.wait_ge(s["uready"], 18 * g + 9 + 3 * m + n + 1)
                            act.activation(gate[:, m, unit(n)], bank[((m + 1) % 2) * 3 + n][:, 0:TT],
                                           ACT.Silu).then_inc(s["uevac"], 1)
                    if g < GROUPS - 1:
                        part(2 * g + 3)

            @block.vector
            def _(dve):
                done = [0]

                def step(ins):
                    done[0] += 1
                    ins.then_inc(s["sums"], 1)

                def rest(j):
                    dve.wait_ge(s["whi"], j + 1)
                    dve.tensor_tensor(w_lo[j % 2][:, :, :], w[j % 2][:, :, :], w_hi[j % 2][:, :, :].bitcast(F32),
                                      ALU.subtract).then_inc(s["wlo"], 1)
                dve.memset(up[:, :, 0:HIST], 0.0).then_inc(s["zeroed"], 1)
                dve.nop().then_inc(s["mixed"], 9)
                rest(0)
                rest(1)
                for g, window in enumerate(WINDOWS):
                    dve.wait_ge(s["sturned"], g + 1)
                    if g:
                        dve.wait_ge(s["tailt"], 2 * g)
                    dve.tensor_copy(us[:, :, :, 0:HIST], aux[1][:, 0:GB * NB_S * HIST].rearrange(
                        "p (m b s) -> p m b s", m=GB, b=NB_S)).then_inc(s["zeroed"], 1)
                    dve.wait_ge(s["zeroed"], g + 2)
                    dve.wait_ge(s["uevac"], 18 * g + 9)
                    if g:
                        dve.wait_ge(s["mready"], 9 * g)
                    for m in range(GB):
                        a, sa, span, side = up[:, m, :], us[:, m, :, :], 1, 0
                        while span < window:
                            b, sb_ = sums[side][:, :], ssum[side][:, :, :]
                            r = 2 * span - 1
                            dve.tensor_tensor(b[:, r:EXT], a[:, r:EXT], a[:, r - span:EXT - span], ALU.add)
                            step(dve.tensor_tensor(sb_[:, :, r:SX], sa[:, :, r:SX], sa[:, :, r - span:SX - span], ALU.add))
                            dve.wait_ge(s["sums"], done[0])
                            a, sa, span, side = b, sb_, 2 * span, 1 - side
                        step(dve.tensor_tensor(a[:, HIST:HIST + 16], a[:, HIST:HIST + 16], c["short"][:, g, :], ALU.mult))
                        dve.wait_ge(s["sums"], done[0])
                        dve.scalar_tensor_tensor(out=pooledT[:, m, 0:SEQ], in0=a[:, HIST:EXT], scalar=1.0 / window,
                                                 in1=up[:, m, HIST:EXT], op0=ALU.mult, op1=ALU.subtract)
                        ins = dve.scalar_tensor_tensor(
                            out=pooledT[:, m, SEQ:T].rearrange("p (b t) -> p b t", t=T_S), in0=sa[:, :, HIST:SX],
                            scalar=1.0 / window, in1=us[:, m, :, HIST:SX], op0=ALU.mult, op1=ALU.subtract)
                        if m < GB - 1:
                            step(ins)
                            dve.wait_ge(s["sums"], done[0])
                    ins.then_inc(s["pooled"], 1)
                    if g < GROUPS - 1:
                        rest(2 * g + 2)
                    for e in range(2):
                        dve.wait_ge(s["tailt"], 2 * g + e + 1)
                        if g:
                            dve.wait_ge(s["stored"], 32 * g)
                        rows = HIST if e == 0 else SAMPLES
                        dve.tensor_copy(tail[0:rows, e, :], aux[e][0:rows, 0:GW]).then_inc(s["tailc"], 1)
                    for m in range(GB):
                        for n in range(NT):
                            dve.wait_ge(s["mready"], 9 * g + 3 * m + n + 1)
                            dve.wait_ge(s["uevac"], 18 * g + 9 + 3 * m + n + 1)
                            dve.scalar_tensor_tensor(out=gate[:, m, unit(n)], in0=bank[(m % 2) * 3 + n][:, 0:TT],
                                                     scalar=c["vec"][:, 32 + GB * g + m:33 + GB * g + m],
                                                     in1=gate[:, m, unit(n)], op0=ALU.mult, op1=ALU.mult).then_inc(s["mixed"], 1)
                    if g < GROUPS - 1:
                        rest(2 * g + 3)

            @block.tensor
            def _(pe):
                pe.wait_ge(s["stl"], 16)
                for g in range(GROUPS):
                    if g:
                        pe.wait_ge(s["tailc"], 2 * g)
                    for m in range(GB):
                        ins = pe.transpose(aux[1][:, m * NB_S * HIST:(m + 1) * NB_S * HIST],
                                           state[:, (g * GB + m) * P:(g * GB + m + 1) * P],
                                           c["ident"][0:NB_S * HIST, 0:NB_S * HIST])
                    ins.then_inc(s["sturned"], 1)
                    for half in range(2):
                        pe.wait_ge(s["wlo"], 2 * g + half + 1)
                        for m in range(GB):
                            blk = 3 * half + m
                            for n in range(NT):
                                if blk == 0:
                                    pe.wait_ge(s["mixed"], 9 * g + 7 + n)
                                elif blk > 1:
                                    pe.wait_ge(s["uevac"], 18 * g + 3 * (blk - 2) + n + 1)
                                for kk in range(KD):
                                    ins = product3(pe, bank[(blk % 2) * 3 + n][:, 0:TT],
                                                   w_hi[half][:, kk, m * P:(m + 1) * P], w_lo[half][:, kk, m * P:(m + 1) * P],
                                                   hT_hi[:, kk, unit(n)], hT_lo[:, kk, unit(n)], kk == 0, kk == KD - 1)
                                ins.then_inc(s["uready"], 1)
                    pe.wait_ge(s["pooled"], g + 1)
                    for m in range(GB):
                        ins = pe.transpose(aux[0][0:HIST, m * P:(m + 1) * P], up[:, m, SEQ:SEQ + HIST], c["ident"][:, :])
                    ins.then_inc(s["tailt"], 1)
                    for m in range(GB):
                        ins = pe.transpose(aux[1][0:SAMPLES, m * P:(m + 1) * P], un[:, m, :], c["ident"][:, :])
                    ins.then_inc(s["tailt"], 1)
                    pe.wait_ge(s["wgl"], 16 * (g + 1))
                    for m in range(GB):
                        for n in range(NT):
                            if m < 2:
                                pe.wait_ge(s["uevac"], 18 * g + 12 + 3 * m + n + 1)
                            else:
                                pe.wait_ge(s["mixed"], 9 + 9 * g + n + 1)
                            for kk in range(GB):
                                ins = pe.matmul(bank[(m % 2) * 3 + n][:, 0:TT],
                                                wg[:, kk, m * P:(m + 1) * P],
                                                pooledT[:, kk, unit(n)], start=kk == 0, stop=kk == GB - 1)
                            ins.then_inc(s["mready"], 1)


def memory_attention_phase(nc, c, A, yT, i, w_src, q0, g0, hT_hi, hT_lo):
    with ExitStack() as ctx:
        k = Kit(nc, ctx, f"a{i}_")
        WC = 2 * P
        qT = k.sb("qT", [P, MH, T])
        sq = k.sb("sq", [P, MH, T])
        gate = k.sb("gate", [P, MH, T])
        R = NB_S * MH * T_S
        qpad = k.sb("qpad", [P, NB_S * MH * (R + T_S)])
        sqs = k.sb("sqs", [P, R])
        NC = TILES * MH + 1
        bank = k.ps("bank", 8)
        names = "wl whi wlo ready evac squares padded sqready".split()
        s = {n: k.sem(n) for n in names}
        unit = lambda n: slice(n * TT, (n + 1) * TT)
        with ExitStack() as wctx:
            kw = Kit(nc, wctx, f"aw{i}_")
            w = kw.sb("w", [P, KD, WC])
            w_hi = [kw.sb(f"w_hi{n}", [P, KD, WC], F32R) for n in range(2)]
            w_lo = [kw.sb(f"w_lo{n}", [P, KD, WC], F32R) for n in range(2)]
            block = wctx.enter_context(nc.Block())

            @block.sync
            def _(sp):
                for j in range(4):
                    if j:
                        sp.wait_ge(s["wlo"], j)
                    off = (q0 if j < 2 else g0) + (j % 2) * WC
                    sp.dma_start(w[:, :, :], w_src[:, off:off + WC].rearrange("(k p) n -> p k n", p=P)
                                 ).then_inc(s["wl"], 16)

            @block.gpsimd
            def _(gp):
                gp.memset(qpad[:, :], 0.0).then_inc(s["padded"], 1)
                gp.wait_ge(s["padded"], 1)
                qv = qpad[:, :].rearrange("p (b h c) -> p b h c", b=NB_S, h=MH)
                sv = sqs[:, :].rearrange("p (b h t) -> p b h t", b=NB_S, h=MH)
                for h in range(MH):
                    gp.wait_ge(s["evac"], 3 * h + 3)
                    gp.tensor_tensor(sq[:, h, :], qT[:, h, :], qT[:, h, :], ALU.mult).then_inc(s["squares"], 1)
                    gp.tensor_copy(qv[:, :, h, 0:T_S], qT[:, h, SEQ:T].rearrange("p (b t) -> p b t", t=T_S)
                                   ).then_inc(s["padded"], 1)
                    gp.wait_ge(s["squares"], h + 1)
                    gp.tensor_copy(sv[:, :, h, :], sq[:, h, SEQ:T].rearrange("p (b t) -> p b t", t=T_S)
                                   ).then_inc(s["sqready"], 1)

            @block.scalar
            def _(act):
                def part(j):
                    act.wait_ge(s["wl"], 16 * (j + 1))
                    if j >= 2:
                        act.wait_ge(s["ready"], 6 * (j - 1))
                    act.activation(w_hi[j % 2][:, :, :], w[:, :, :], ACT.Copy).then_inc(s["whi"], 1)
                part(0)
                part(1)
                for blk in range(2 * MH):
                    for n in range(NT):
                        act.wait_ge(s["ready"], 3 * blk + n + 1)
                        src = bank[(blk % 2) * 3 + n][:, 0:TT]
                        if blk < MH:
                            ins = act.activation(qT[:, blk, unit(n)], src, ACT.Copy)
                        else:
                            ins = act.activation(gate[:, blk - MH, unit(n)], src, ACT.Silu)
                        ins.then_inc(s["evac"], 1)
                    if blk in (1, 3):
                        part(2 + blk // 2)

            @block.vector
            def _(dve):
                def rest(j):
                    dve.wait_ge(s["whi"], j + 1)
                    dve.tensor_tensor(w_lo[j % 2][:, :, :], w[:, :, :], w_hi[j % 2][:, :, :].bitcast(F32),
                                      ALU.subtract).then_inc(s["wlo"], 1)
                for j in range(4):
                    rest(j)

            @block.tensor
            def _(pe):
                for blk in range(2 * MH):
                    j = blk // 2
                    pe.wait_ge(s["wlo"], j + 1)
                    for n in range(NT):
                        if blk >= 2:
                            pe.wait_ge(s["evac"], 3 * (blk - 2) + n + 1)
                        for kk in range(KD):
                            m = blk % 2
                            ins = product3(pe, bank[(blk % 2) * 3 + n][:, 0:TT], w_hi[j % 2][:, kk, m * P:(m + 1) * P],
                                           w_lo[j % 2][:, kk, m * P:(m + 1) * P], hT_hi[:, kk, unit(n)],
                                           hT_lo[:, kk, unit(n)], kk == 0, kk == KD - 1)
                        ins.then_inc(s["ready"], 1)
        st = k.sb("st", [P, 4, NC])
        mk = k.sb("mk", [P, 2, MJ, MW])
        mkT = k.sb("mkT", [P, 2, MH, MEM])
        mv = k.sb("mv", [P, 2, MJ, MW])
        mx = k.sb("mx", [P, 2, MH])
        nb = k.sb("nb", [P, 2, MH])
        sums = k.sb("sums", [P, 2, MH])
        rsum = k.sb("rsum", [P, 2, MH])
        e = k.sb("e", [P, 2, MH, MEM])
        pT = k.sb("pT", [P, MH, MJ, P])
        sx = k.sb("sx", [P, 4])
        es = k.sb("es", [P, MEM])
        psT = k.sb("psT", [P, MJ, R])
        kl = [k.sem(f"kl{n}") for n in range(2)]
        vl = [k.sem(f"vl{n}") for n in range(2)]
        names = ("msq mean root inv rs ktr kev ksc score mxs nbs ex rec nrm "
                 "tr ptA ptD pv ym smx snb sex srec snrm str_ spt spv sym stored").split()
        s.update({n: k.sem(n) for n in names})

        def turned_probs(act, t):
            act.wait_ge(s["tr"], 2 * t + 1)
            if t >= 1:
                act.wait_ge(s["pv"], t)
            act.activation(pT[:, 0:2, :, :], bank[4][:, :].rearrange("p (h j q) -> p h j q", h=2, j=MJ),
                           ACT.Copy).then_inc(s["ptA"], 1)

        with nc.Block() as block:
            @block.sync
            def _(sp):
                for b in range(NB_S):
                    if b >= 2:
                        sp.wait_ge(s["ktr"], 2 * (b - 1))
                    sp.dma_start(mk[:, b % 2, :, :], A["cache_mem_k"][i, b].rearrange("(j p) h d -> p j (h d)", p=P)
                                 ).then_inc(kl[b % 2], 16)
                for b in range(NB_S):
                    if b >= 2:
                        sp.wait_ge(s["spv"], b - 1)
                    sp.dma_start(mv[:, b % 2, :, :], A["cache_mem_v"][i, b].rearrange("(j p) h d -> p j (h d)", p=P)
                                 ).then_inc(vl[b % 2], 16)
                sp.wait_ge(s["ym"], TILES)
                sp.wait_ge(s["sym"], 1)
                for h in range(MH):
                    sp.dma_start(yT[HEADS + h], gate[:, h, :]).then_inc(s["stored"], 16)
                sp.wait_ge(s["stored"], 16 * MH)

            @block.scalar
            def _(act):
                act.wait_ge(s["mean"], 1)
                act.activation(st[:, 1, :], st[:, 0, :], ACT.Sqrt).then_inc(s["root"], 1)
                for b in range(NB_S):
                    act.wait_ge(s["ktr"], 2 * b + 2)
                    if b >= 2:
                        act.wait_ge(s["ksc"], b - 1)
                    act.activation(mkT[:, b % 2, 2:4, :], bank[5][:, :].rearrange("p (h m) -> p h m", h=2), ACT.Identity,
                                   scale=c["vec"][:, 44 + i:45 + i]).then_inc(s["kev"], 1)
                act.wait_ge(s["snb"], 1)
                act.activation(es[:, :], bank[7][:, 0:MEM], ACT.Exp, bias=sx[:, 1:2], scale=st[:, 3, NC - 1:NC],
                               accum_out=sx[:, 2:3]).then_inc(s["sex"], 1)
                for t in range(TILES):
                    act.wait_ge(s["nbs"], t + 1)
                    if t >= 2:
                        act.wait_ge(s["tr"], 2 * (t - 1))
                    for h in range(MH):
                        act.activation(e[:, t % 2, h, :], bank[2 * (t % 2) + h // 2][:, (h % 2) * MEM:(h % 2 + 1) * MEM],
                                       ACT.Exp, bias=nb[:, t % 2, h:h + 1], scale=st[:, 3, t * MH + h:t * MH + h + 1],
                                       accum_out=sums[:, t % 2, h:h + 1]).then_inc(s["ex"], 1)
                    if t >= 1:
                        turned_probs(act, t - 1)
                turned_probs(act, TILES - 1)
                act.wait_ge(s["str_"], 1)
                act.activation(psT[:, :, :], bank[7][:, MEM:2 * MEM].rearrange("p (j r) -> p j r", j=MJ),
                               ACT.Copy).then_inc(s["spt"], 1)

            @block.vector
            def _(dve):
                dve.wait_ge(s["msq"], 1)
                dve.tensor_scalar(st[:, 0, :], bank[7][:, 0:NC], 1.0 / HD, EPS, ALU.mult, ALU.add).then_inc(s["mean"], 1)
                dve.wait_ge(s["root"], 1)
                dve.reciprocal(st[:, 2, :], st[:, 1, :]).then_inc(s["inv"], 1)
                dve.wait_ge(s["inv"], 1)
                dve.tensor_scalar(st[:, 3, :], st[:, 2, :], SCALE, None, ALU.mult).then_inc(s["rs"], 1)
                for b in range(NB_S):
                    dve.wait_ge(s["ktr"], 2 * b + 1)
                    if b >= 2:
                        dve.wait_ge(s["ksc"], b - 1)
                    dve.tensor_scalar(mkT[:, b % 2, 0:2, :], bank[4][:, :].rearrange("p (h m) -> p h m", h=2),
                                      c["vec"][:, 44 + i:45 + i], None, ALU.mult).then_inc(s["kev"], 1)
                dve.wait_ge(s["ksc"], NB_S)
                dve.reduce_max(sx[:, 0:1], bank[7][:, 0:MEM], AX_X).then_inc(s["smx"], 1)
                dve.wait_ge(s["rs"], 1)
                dve.wait_ge(s["smx"], 1)
                dve.scalar_tensor_tensor(out=sx[:, 1:2], in0=sx[:, 0:1], scalar=-1.0, in1=st[:, 3, NC - 1:NC],
                                         op0=ALU.mult, op1=ALU.mult).then_inc(s["snb"], 1)

                def maxima(t):
                    for half in range(2):
                        dve.wait_ge(s["score"], 2 * t + half + 1)
                        ins = dve.reduce_max(mx[:, t % 2, 2 * half:2 * half + 2],
                                             bank[2 * (t % 2) + half][:, :].rearrange("p (h m) -> p h m", h=2), AX_X)
                    ins.then_inc(s["mxs"], 1)
                    dve.wait_ge(s["mxs"], t + 1)
                    if t >= 2:
                        dve.wait_ge(s["ex"], MH * (t - 1))
                    dve.scalar_tensor_tensor(out=nb[:, t % 2, :], in0=mx[:, t % 2, :], scalar=-1.0,
                                             in1=st[:, 3, t * MH:(t + 1) * MH], op0=ALU.mult, op1=ALU.mult
                                             ).then_inc(s["nbs"], 1)

                def weights(t):
                    dve.wait_ge(s["ex"], MH * (t + 1))
                    dve.reciprocal(rsum[:, t % 2, :], sums[:, t % 2, :]).then_inc(s["rec"], 1)
                    dve.wait_ge(s["rec"], t + 1)
                    for h in range(MH):
                        ins = dve.tensor_scalar(e[:, t % 2, h, :], e[:, t % 2, h, :], rsum[:, t % 2, h:h + 1], None, ALU.mult)
                    ins.then_inc(s["nrm"], 1)

                def gated(t):
                    dve.wait_ge(s["pv"], t + 1)
                    tile = slice(t * P, (t + 1) * P)
                    dve.tensor_tensor(gate[:, :, tile], bank[6][:, :].rearrange("p (h q) -> p h q", h=MH),
                                      gate[:, :, tile], ALU.mult).then_inc(s["ym"], 1)
                maxima(0)
                dve.wait_ge(s["sex"], 1)
                dve.reciprocal(sx[:, 3:4], sx[:, 2:3]).then_inc(s["srec"], 1)
                dve.wait_ge(s["srec"], 1)
                dve.tensor_scalar(es[:, :], es[:, :], sx[:, 3:4], None, ALU.mult).then_inc(s["snrm"], 1)
                for t in range(TILES):
                    if t + 1 < TILES:
                        maxima(t + 1)
                    weights(t)
                    dve.wait_ge(s["tr"], 2 * t + 2)
                    if t >= 1:
                        dve.wait_ge(s["pv"], t)
                    dve.tensor_copy(pT[:, 2:4, :, :], bank[5][:, :].rearrange("p (h j q) -> p h j q", h=2, j=MJ)
                                    ).then_inc(s["ptD"], 1)
                    gated(t)
                dve.wait_ge(s["spv"], NB_S)
                for h in range(MH):
                    o = bank[7][:, 0:R].rearrange("p (b h t) -> p b h t", b=NB_S, h=MH)[:, :, h, :]
                    g = gate[:, h, SEQ:T].rearrange("p (b t) -> p b t", t=T_S)
                    ins = dve.tensor_tensor(g, o, g, ALU.mult)
                ins.then_inc(s["sym"], 1)

            @block.tensor
            def _(pe):
                pe.wait_ge(s["sqready"], MH)
                for t in range(TILES):
                    for h in range(MH):
                        pe.matmul(bank[7][:, t * MH + h:t * MH + h + 1], sq[:, h, t * P:(t + 1) * P],
                                  c["ones"][:, 0:1], start=True, stop=True)
                pe.matmul(bank[7][:, NC - 1:NC], sqs[:, :], c["ones"][:, 0:1], start=True, stop=True).then_inc(s["msq"], 1)
                pe.wait_ge(s["evac"], 6 * MH)
                pe.wait_ge(s["padded"], MH + 1)
                pe.wait_ge(s["mean"], 1)

                def turn_keys(b):
                    pe.wait_ge(kl[b % 2], 16 * (b // 2 + 1))
                    if b >= 1:
                        pe.wait_ge(s["kev"], 2 * b)
                    for q in range(2):
                        for hh in range(2):
                            for j in range(MJ):
                                h = 2 * q + hh
                                ins = pe.transpose(bank[4 + q][:, hh * MEM + j * P:hh * MEM + (j + 1) * P],
                                                   mk[:, b % 2, j, h * HD:(h + 1) * HD], c["ident"][:, :])
                        ins.then_inc(s["ktr"], 1)

                def sample_scores(b):
                    pe.wait_ge(s["kev"], 2 * b + 2)
                    for h in range(MH):
                        x = b * MH + h
                        ins = pe.matmul(bank[7][:, 0:MEM], qpad[:, x * R:(x + 1) * R], mkT[:, b % 2, h, :],
                                        start=x == 0, stop=x == NB_S * MH - 1)
                    ins.then_inc(s["ksc"], 1)
                turn_keys(0)
                for b in range(NB_S):
                    if b + 1 < NB_S:
                        turn_keys(b + 1)
                    sample_scores(b)

                def scores(t):
                    if t >= 2:
                        pe.wait_ge(s["ex"], MH * (t - 1))
                    for h in range(MH):
                        ins = pe.matmul(bank[2 * (t % 2) + h // 2][:, (h % 2) * MEM:(h % 2 + 1) * MEM],
                                        qT[:, h, t * P:(t + 1) * P], c["mkT"][:, h, :], start=True, stop=True)
                        if h % 2:
                            ins.then_inc(s["score"], 1)
                scores(0)
                for t in range(TILES):
                    if t + 1 < TILES:
                        scores(t + 1)
                    pe.wait_ge(s["nrm"], t + 1)
                    if t >= 1:
                        pe.wait_ge(s["ptA"], t)
                        pe.wait_ge(s["ptD"], t)
                    else:
                        pe.wait_ge(s["kev"], 2 * NB_S)
                    for q in range(2):
                        for hh in range(2):
                            for j in range(MJ):
                                ins = pe.transpose(bank[4 + q][:, (hh * MJ + j) * P:(hh * MJ + j + 1) * P],
                                                   e[:, t % 2, 2 * q + hh, j * P:(j + 1) * P], c["ident"][:, :])
                        ins.then_inc(s["tr"], 1)
                    pe.wait_ge(s["ptA"], t + 1)
                    pe.wait_ge(s["ptD"], t + 1)
                    if t >= 1:
                        pe.wait_ge(s["ym"], t)
                    for h in range(MH):
                        for j in range(MJ):
                            ins = pe.matmul(bank[6][:, h * P:(h + 1) * P], c["mv"][:, j, h * HD:(h + 1) * HD],
                                            pT[:, h, j, :], start=j == 0, stop=j == MJ - 1)
                    ins.then_inc(s["pv"], 1)
                pe.wait_ge(s["snrm"], 1)
                for j in range(MJ):
                    ins = pe.transpose(bank[7][:, MEM + j * R:MEM + (j + 1) * R], es[:, j * P:(j + 1) * P], c["ident"][:, :])
                ins.then_inc(s["str_"], 1)
                pe.wait_ge(s["spt"], 1)
                for b in range(NB_S):
                    pe.wait_ge(vl[b % 2], 16 * (b // 2 + 1))
                    for h in range(MH):
                        x = (b * MH + h) * T_S
                        for j in range(MJ):
                            ins = pe.matmul(bank[7][:, x:x + T_S], mv[:, b % 2, j, h * HD:(h + 1) * HD],
                                            psT[:, j, x:x + T_S], start=j == 0, stop=j == MJ - 1)
                    ins.then_inc(s["spv"], 1)


def out_phase(nc, c, A, yT, i, source, target):
    with ExitStack() as ctx:
        k = Kit(nc, ctx, f"o{i}_")
        KM = 2 * D // P
        CH = 2
        w = [k.sb(f"w{n}", [P, CH, D]) for n in range(2)]
        w_hi = k.sb("w_hi", [P, KM, D], F32R)
        w_lo = k.sb("w_lo", [P, KM, D], F32R)
        y = k.sb("y", [P, KM, P])
        y_hi = [k.sb(f"y_hi{n}", [P, KM, P], F32R) for n in range(2)]
        y_lo = [k.sb(f"y_lo{n}", [P, KM, P], F32R) for n in range(2)]
        x = k.sb("x", [P, 2, D])
        bank = k.ps("bank", 4)
        wl = [k.sem(f"wl{n}") for n in range(2)]
        xl = [k.sem(f"xl{n}") for n in range(2)]
        ol = [k.sem(f"ol{n}") for n in range(2)]
        s = {n: k.sem(n) for n in "yl whi wlo yhi ylo ready added".split()}
        N = TILES + 1
        NW = KM // CH
        tok = lambda t: t * P if t < TILES else LAST
        with nc.Block() as block:
            @block.sync
            def _(sp):
                def load_y(t):
                    if t:
                        sp.wait_ge(s["ylo"], t)
                    sp.dma_start(y[:, :, :], yT[:, :, tok(t):tok(t) + P].rearrange("k p t -> p k t")).then_inc(s["yl"], 16)
                    if t >= 2:
                        sp.wait_ge(ol[t % 2], 16 * (t // 2))
                    pieces = source(t)
                    for r0, r1, src in pieces:
                        sp.dma_start(x[r0:r1, t % 2, :], src).then_inc(xl[t % 2], 32 // len(pieces))
                load_y(0)
                for j in range(NW):
                    if j >= 2:
                        sp.wait_ge(s["wlo"], j - 1)
                    sp.dma_start(w[j % 2][:, :, :], A["w_out"][i, j * CH * P:(j + 1) * CH * P, :].rearrange(
                        "(k p) n -> p k n", p=P)).then_inc(wl[j % 2], 16)
                load_y(1)
                for t in range(N):
                    sp.wait_ge(s["added"], 2 * t + 2)
                    r0, r1, dst = target(t)
                    sp.dma_start(dst, x[r0:r1, t % 2, :]).then_inc(ol[t % 2], 16)
                    if t + 2 < N:
                        load_y(t + 2)
                for n in range(2):
                    sp.wait_ge(ol[n], 16 * ((N - n + 1) // 2))

            @block.scalar
            def _(act):
                def part(t):
                    act.wait_ge(s["yl"], 16 * (t + 1))
                    if t >= 2:
                        act.wait_ge(s["ready"], 2 * (t - 1))
                    act.activation(y_hi[t % 2][:, :, :], y[:, :, :], ACT.Copy).then_inc(s["yhi"], 1)
                part(0)
                for j in range(NW):
                    act.wait_ge(wl[j % 2], 16 * (j // 2 + 1))
                    act.activation(w_hi[:, j * CH:(j + 1) * CH, :], w[j % 2][:, :, :], ACT.Copy).then_inc(s["whi"], 1)
                for t in range(1, N):
                    part(t)

            @block.vector
            def _(dve):
                def rest(t):
                    dve.wait_ge(s["yhi"], t + 1)
                    dve.tensor_tensor(y_lo[t % 2][:, :, :], y[:, :, :], y_hi[t % 2][:, :, :].bitcast(F32),
                                      ALU.subtract).then_inc(s["ylo"], 1)
                rest(0)
                for j in range(NW):
                    dve.wait_ge(s["whi"], j + 1)
                    dve.tensor_tensor(w_lo[:, j * CH:(j + 1) * CH, :], w[j % 2][:, :, :],
                                      w_hi[:, j * CH:(j + 1) * CH, :].bitcast(F32), ALU.subtract).then_inc(s["wlo"], 1)
                for t in range(N):
                    if t + 1 < N:
                        rest(t + 1)
                    dve.wait_ge(xl[t % 2], 32 * (t // 2 + 1))
                    for half in range(2):
                        dve.wait_ge(s["ready"], 2 * t + half + 1)
                        a = x[:, t % 2, half * 512:(half + 1) * 512]
                        dve.tensor_tensor(a, bank[2 * (t % 2) + half][:, :], a, ALU.add).then_inc(s["added"], 1)

            @block.tensor
            def _(pe):
                for t in range(N):
                    pe.wait_ge(s["ylo"], t + 1)
                    if t >= 2:
                        pe.wait_ge(s["added"], 2 * (t - 1))
                    for kk in range(KM):
                        if t == 0 and kk % CH == 0:
                            pe.wait_ge(s["wlo"], kk // CH + 1)
                        for half in range(2):
                            n = slice(half * 512, (half + 1) * 512)
                            ins = product3(pe, bank[2 * (t % 2) + half][:, :], y_hi[t % 2][:, kk, :], y_lo[t % 2][:, kk, :],
                                           w_hi[:, kk, n], w_lo[:, kk, n], kk == 0, kk == KM - 1)
                            if kk == KM - 1:
                                ins.then_inc(s["ready"], 1)


def in_phase(nc, c, A, O, S, hT_hi, hT_lo):
    with ExitStack() as ctx:
        k = Kit(nc, ctx, "i_")
        w = [k.sb(f"w{n}", [P, KD, KU]) for n in range(2)]
        w_hi = [k.sb(f"w_hi{n}", [P, KD, KU], F32R) for n in range(2)]
        w_lo = [k.sb(f"w_lo{n}", [P, KD, KU], F32R) for n in range(2)]
        stage = k.sb("stage", [P, 2, T])
        krows = k.sb("krows", [P, 2, TILES, P])
        knew = k.sb("knew", [SAMPLES, 2, P])
        VR = 4
        vrows = k.sb("vrows", [P, VR, KU])
        bank = k.ps("bank", 6)
        aux = k.ps("aux", 2)
        wl = [k.sem(f"wl{n}") for n in range(2)]
        sl = [k.sem(f"sl{n}") for n in range(2)]
        kl = [k.sem(f"kl{n}") for n in range(2)]
        vl = [k.sem(f"vl{n}") for n in range(VR)]
        s = {n: k.sem(n) for n in "whi wlo ready evac turned rowed vready vevac".split()}
        w_src = A["w_in_sb"][0]
        kinds = ["q"] * 4 + ["k"] * 4 + ["gate"] * 4 + ["v"] * 4
        base = {"q": 0, "k": BW, "v": 2 * BW, "gate": 3 * BW}
        chunks = [(kind, base[kind] + (j % 4) * KU) for j, kind in enumerate(kinds)]
        blocks = [(kind, (j % 4) * GB + m) for j, kind in enumerate(kinds[:12]) for m in range(GB)]
        kblocks = [b for b, (kind, _) in enumerate(blocks) if kind == "k"]
        target = {"q": S["qT"], "k": S["kT"], "gate": S["gT"]}
        N = TILES + 1
        tok = lambda t: t * P if t < TILES else LAST
        unit = lambda n: slice(n * TT, (n + 1) * TT)
        VU = 4 * N

        def store_krows(eng, b):
            h = blocks[b][1]
            n = b - kblocks[0]
            eng.wait_ge(s["rowed"], 3 * n + 3)
            eng.dma_start(O["sbk_p"][0, 0, :, h, :].rearrange("(t p) d -> p t d", p=P), krows[:, n % 2, :, :]
                          ).then_inc(kl[n % 2], 16)
            eng.dma_start(O["sbk_s"][0, :, :, h, :].rearrange("b t d -> (b t) d"), knew[:, n % 2, :]
                          ).then_inc(kl[n % 2], 16)

        with nc.Block() as block:
            @block.sync
            def _(sp):
                def load(j):
                    if j >= 2:
                        sp.wait_ge(s["wlo"], j - 1)
                    sp.dma_start(w[j % 2][:, :, :], w_src[:, chunks[j][1]:chunks[j][1] + KU].rearrange(
                        "(k p) n -> p k n", p=P)).then_inc(wl[j % 2], 16)
                load(0)
                load(1)
                for b, (kind, h) in enumerate(blocks):
                    if b % GB == 1 and b // GB + 2 < 16:
                        load(b // GB + 2)
                    sp.wait_ge(s["evac"], 3 * b + 3)
                    sp.dma_start(target[kind][h], stage[:, b % 2, :]).then_inc(sl[b % 2], 16)
                    if b - 1 in kblocks:
                        store_krows(sp, b - 1)
                load(14)
                load(15)

            @block.gpsimd
            def _(gp):
                for u in range(VU):
                    j, t = u // N, u % N
                    gp.wait_ge(s["vevac"], u + 1)
                    cols = slice(j * KU, (j + 1) * KU)
                    if t < TILES:
                        dst = O["sbv_p"][0, 0, t * P:(t + 1) * P].rearrange("s h d -> s (h d)")[:, cols]
                        gp.dma_start(dst, vrows[:, u % VR, :]).then_inc(vl[u % VR], 16)
                    else:
                        dst = O["sbv_s"][0].rearrange("b t h d -> (b t) (h d)")[:, cols]
                        gp.dma_start(dst, vrows[P - SAMPLES:P, u % VR, :]).then_inc(vl[u % VR], 16)
                for n in range(VR):
                    gp.wait_ge(vl[n], 16 * (VU // VR))
                for n in range(2):
                    gp.wait_ge(sl[n], 16 * len(blocks) // 2)
                    gp.wait_ge(kl[n], 32 * len(kblocks) // 2)

            @block.scalar
            def _(act):
                def part(j):
                    act.wait_ge(wl[j % 2], 16 * (j // 2 + 1))
                    if j >= 2:
                        act.wait_ge(s["ready"], min(9 * (j - 1), 3 * len(blocks)))
                        if j - 2 >= 12:
                            act.wait_ge(s["vready"], N * (j - 13))
                    act.activation(w_hi[j % 2][:, :, :], w[j % 2][:, :, :], ACT.Copy).then_inc(s["whi"], 1)
                part(0)
                part(1)
                for b, (kind, h) in enumerate(blocks):
                    for n in range(NT):
                        act.wait_ge(s["ready"], 3 * b + n + 1)
                        if n == 0 and b >= 2:
                            act.wait_ge(sl[b % 2], 16 * (b // 2))
                            if b - 2 in kblocks:
                                act.wait_ge(s["turned"], 3 * (b - 2 - kblocks[0]) + 3)
                        act.activation(stage[:, b % 2, unit(n)], bank[(b % 2) * 3 + n][:, 0:TT],
                                       ACT.Silu if kind == "gate" else ACT.Copy).then_inc(s["evac"], 1)
                    if b % GB == GB - 1:
                        part(b // GB + 2)
                for u in range(0, VU):
                    if u % N == N - 1 and u // N + 14 < 16:
                        part(u // N + 14)

            @block.vector
            def _(dve):
                def rest(j):
                    dve.wait_ge(s["whi"], j + 1)
                    dve.tensor_tensor(w_lo[j % 2][:, :, :], w[j % 2][:, :, :], w_hi[j % 2][:, :, :].bitcast(F32),
                                      ALU.subtract).then_inc(s["wlo"], 1)
                rest(0)
                rest(1)
                for b, (kind, h) in enumerate(blocks):
                    if b % GB == 0 and b:
                        rest(b // GB + 1)
                    if kind == "k":
                        n = b - kblocks[0]
                        if n >= 2:
                            dve.wait_ge(kl[n % 2], 32 * (n // 2))
                        for q in range(2):
                            dve.wait_ge(s["turned"], 3 * n + q + 1)
                            dve.tensor_copy(krows[:, n % 2, 4 * q:4 * q + 4, :],
                                            aux[q][:, :].rearrange("p (t d) -> p t d", t=4)).then_inc(s["rowed"], 1)
                        dve.wait_ge(s["turned"], 3 * n + 3)
                        dve.tensor_copy(knew[:, n % 2, :], aux[0][0:SAMPLES, 0:P]).then_inc(s["rowed"], 1)
                rest(13)
                for u in range(VU):
                    dve.wait_ge(s["vready"], u + 1)
                    if u >= VR:
                        dve.wait_ge(vl[u % VR], 16 * (u // VR))
                    dve.tensor_copy(vrows[:, u % VR, :], bank[u % 6][:, 0:KU]).then_inc(s["vevac"], 1)
                    if u % N == N - 1 and u // N + 14 < 16:
                        rest(u // N + 14)

            @block.tensor
            def _(pe):
                def turn_keys(b):
                    n = b - kblocks[0]
                    pe.wait_ge(s["evac"], 3 * b + 3)
                    if n:
                        pe.wait_ge(s["rowed"], 3 * n)
                    for q in range(2):
                        for t in range(4):
                            ins = pe.transpose(aux[q][:, t * P:(t + 1) * P],
                                               stage[:, b % 2, (4 * q + t) * P:(4 * q + t + 1) * P], c["ident"][:, :])
                        ins.then_inc(s["turned"], 1)
                    pe.wait_ge(s["rowed"], 3 * n + 1)
                    pe.transpose(aux[0][0:SAMPLES, 0:P], stage[:, b % 2, SEQ:T], c["ident"][:, :]).then_inc(s["turned"], 1)
                for b, (kind, h) in enumerate(blocks):
                    j, m = b // GB, b % GB
                    if m == 0:
                        pe.wait_ge(s["wlo"], j + 1)
                    for n in range(NT):
                        if b >= 2:
                            pe.wait_ge(s["evac"], 3 * (b - 2) + n + 1)
                        for kk in range(KD):
                            ins = product3(pe, bank[(b % 2) * 3 + n][:, 0:TT], w_hi[j % 2][:, kk, m * P:(m + 1) * P],
                                           w_lo[j % 2][:, kk, m * P:(m + 1) * P], hT_hi[:, kk, unit(n)],
                                           hT_lo[:, kk, unit(n)], kk == 0, kk == KD - 1)
                        ins.then_inc(s["ready"], 1)
                        if n == 0 and b - 1 in kblocks:
                            turn_keys(b - 1)
                pe.wait_ge(s["evac"], 3 * len(blocks))
                for u in range(VU):
                    j, t = 12 + u // N, u % N
                    if t == 0:
                        pe.wait_ge(s["wlo"], j + 1)
                    if u >= 6:
                        pe.wait_ge(s["vevac"], u - 5)
                    for kk in range(KD):
                        a = slice(tok(t), tok(t) + P)
                        ins = product3(pe, bank[u % 6][:, 0:KU], hT_hi[:, kk, a], hT_lo[:, kk, a],
                                       w_hi[j % 2][:, kk, :], w_lo[j % 2][:, kk, :], kk == 0, kk == KD - 1)
                    ins.then_inc(s["vready"], 1)


def stick_phase(nc, c, A, O, S):
    ITERS, HI, BI = 4, HEADS // 4, NB_S // 4
    PG = 4
    HH = HEADS // 2
    Q = P // PG
    GC = HEADS * PG * T_S
    UR = HH * PG * T_S
    VC = 512
    NSTEP = 12 * HI
    steps = []
    for hh in range(HI):
        for ch in range(2):
            for kb in range(4 * ch + 3, -1, -1):
                first_q = max(kb * P, ch * 512)
                steps.append((hh, ch, kb, first_q, (ch + 1) * 512 - first_q, kb >= 4 * ch, kb == 4 * ch + 3, kb == 0))
    order = []
    for bb in range(BI):
        p0 = bb * NSTEP // BI
        for u in range(8):
            order.append(("K", bb, u))
            order.append(("T", bb, u - 1) if u else ("S", bb - 1, 0))
            order.append(("P", p0 + u))
        order += [("T", bb, 7), ("P", p0 + 8), ("P", p0 + 9), ("C", bb, 0), ("P", p0 + 10)]
        for v in range(PAGES):
            order.append(("V", bb, v))
            if v % 2 and v < 14:
                order.append(("P", p0 + 11 + v // 2))
    order = [e for e in order if e != ("S", -1, 0)]
    with ExitStack() as ctx:
        k = Kit(nc, ctx, "b_")
        qh = k.sb("qh", [P, HI, SEQ])
        kh = k.sb("kh", [P, HI, SEQ])
        vh = k.sb("vh", [P, HI, TILES, HD])
        gh = k.sb("gh", [P, HI, SEQ])
        z = k.sb("z", [P, 3, 512])
        soft = k.sb("soft", [P, 2, 512])
        spl = k.sb("spl", [P, 3, 512])
        a = k.sb("a", [P, 3, 512])
        kraw = [k.sb(f"kraw{n}", [P, PG, HH * HD]) for n in range(2)]
        kt = [k.sb(f"kt{n}", [P, HH, HD // Q, P]) for n in range(2)]
        vpage = [k.sb(f"vpage{n}", [P, BW]) for n in range(4)]
        qs = k.sb("qs", [P, HEADS * PG, SAMPLES])
        qd = k.sb("qd", [P, HEADS * PG * UR + UR])
        kev = k.sb("kev", [UR, 2, P])
        vev = k.sb("vev", [HEADS * T_S, BW])
        onew = k.sb("onew", [P, HEADS, SAMPLES])
        dz = k.sb("dz", [P, 4 * GC])
        dx = k.sb("dx", [P, 4 * GC])
        dsp = k.sb("dsp", [P, 4 * GC])
        dr = k.sb("dr", [P, 4 * GC])
        da = k.sb("da", [P, 4 * GC])
        daw = k.sb("daw", [P, PAGES, HEADS * T_S])
        pages = k.sb("pages", [1, NB_S * PAGES], I32)
        bias = k.sb("bias", [P, 2, HEADS, PG * T_S])
        nsp = k.sb("nsp", [P, HEADS, SAMPLES])
        bcol = k.sb("bcol", [P, HI])
        gs = k.sb("gs", [P, HEADS, SAMPLES])
        zbank = k.ps("zbank", 2)
        cbank = k.ps("cbank")
        obank = k.ps("obank")
        sbank = k.ps("sbank", 2)
        rbank = k.ps("rbank", 2)
        s = {n: k.sem(n) for n in (
            "pre passed bc qb so zr zev nab ee el spm spr tri tm tsub ax pvd oev ktr kdone dzev dnab dee dl dspr rs rr dc dt "
            "dax vdone ys_end kr rev ve sel").split()}
        kl = [k.sem(f"kl{n}") for n in range(2)]
        vl = [k.sem(f"vl{n}") for n in range(4)]
        hl = [k.sem(f"hl{n}") for n in range(HI)]
        ys = [k.sem(f"ys{n}") for n in range(HI)]
        ND = 8 * HI
        per = dict(zr=NSTEP, zev=NSTEP, nab=NSTEP, ee=NSTEP, el=NSTEP, spm=ND, spr=NSTEP, tri=NSTEP, tm=ND, tsub=NSTEP,
                   ax=NSTEP, pvd=NSTEP, oev=2 * HI, ktr=16, kdone=16, dzev=4, dnab=2, dee=2, dl=2, dspr=2, rs=16 * BI,
                   rr=2, dc=4, dt=4, dax=4 * BI, vdone=32, qb=4 * PG, bc=1, so=2,
                   kr=16, rev=16, ve=3 * BI, sel=BI)
        ahead = dict(zev=2, tsub=3, pvd=3, oev=1, ktr=2, kdone=2, kr=2, rev=2, ve=3, sel=1, dax=1, vdone=4, so=1)

        def wait(eng, i, name, n):
            assert n + ahead.get(name, 0) > 0 or isinstance(i, int), (name, n)
            eng.wait_ge(s[name], i * per[name] + (n + ahead.get(name, 0)))

        new = lambda t, r=P: t[0:r, 0:HEADS * SAMPLES].rearrange("p (h t) -> p h t", h=HEADS)
        kn, qn = new(z[:, 0, :]), new(z[:, 1, :])
        zn, xn, an = (new(a[:, n, :], SAMPLES) for n in range(3))
        vn = vpage[0][0:SAMPLES, :]
        pre = {n: k.sem("n_" + n) for n in "load qload zero z step e l t a".split()}
        NC_ = HEADS * SAMPLES
        with nc.Block() as block:
            @block.sync
            def _(sp):
                sp.dma_start(kn[:, :, :], S["kT"][:, :, SEQ:T].rearrange("h p t -> p h t")).then_inc(pre["load"], 16)
                sp.dma_start(qn[:, :, :], S["qT"][:, :, SEQ:T].rearrange("h p t -> p h t")).then_inc(pre["load"], 16)
                sp.dma_start(gs[:, :, :], S["gT"][:, :, SEQ:T].rearrange("h p t -> p h t")).then_inc(pre["load"], 16)
                sp.dma_start(vn[:, :], O["sbv_s"][0].rearrange("b t h d -> (b t) (h d)")).then_inc(pre["load"], 16)
                sp.dma_start(pages[:, :], A["page_table"].rearrange("(o b) n -> o (b n)", o=1)).then_inc(pre["load"], 16)
                for x in range(PG):
                    sp.dma_start(qs[x * Q:(x + 1) * Q, :, :], S["qT"][:, :, SEQ:T].rearrange(
                        "h (f j) t -> j (h f) t", j=Q)).then_inc(pre["qload"], 16)
                sp.wait_ge(pre["load"], 80)
                sp.wait_ge(pre["qload"], 16 * PG)

            @block.gpsimd
            def _(gp):
                gp.memset(qd[:, :], 0.0).then_inc(pre["zero"], 1)
                gp.memset(nsp[:, :, :], 0.0).then_inc(pre["zero"], 1)

            @block.tensor
            def _(pe):
                pe.wait_ge(pre["load"], 80)
                for h in range(HEADS):
                    ins = pe.matmul(sbank[0][0:SAMPLES, h * SAMPLES:(h + 1) * SAMPLES], kn[:, h, :], qn[:, h, :],
                                    start=True, stop=True)
                ins.then_inc(pre["z"], 1)
                pe.wait_ge(pre["step"], 5 + HEADS)
                pe.matmul(sbank[1][0:SAMPLES, 0:NC_], c["suffix"][0:SAMPLES, 0:SAMPLES],
                          nsp[0:SAMPLES, :, :].rearrange("p h t -> p (h t)"), start=True, stop=True).then_inc(pre["z"], 1)
                pe.wait_ge(pre["a"], 1)
                for h in range(HEADS):
                    ins = pe.matmul(rbank[0][:, h * SAMPLES:(h + 1) * SAMPLES], vn[:, h * HD:(h + 1) * HD], an[:, h, :],
                                    start=True, stop=True)
                ins.then_inc(pre["z"], 1)

            @block.scalar
            def _(act):
                act.preload_act_table_set("natural_log_exp_and_others")
                act.wait_ge(pre["step"], 4)
                act.activation(xn[:, :, :], xn[:, :, :], ACT.Exp).then_inc(pre["e"], 1)
                act.wait_ge(pre["e"], 1)
                act.activation(xn[:, :, :], xn[:, :, :], ACT.Ln, bias=1.0).then_inc(pre["l"], 1)
                act.wait_ge(pre["t"], 1 + HEADS)
                act.activation(an[:, :, :], an[:, :, :], ACT.Exp).then_inc(pre["a"], 1)

            @block.vector
            def _(dve):
                for h in range(HEADS):
                    ins = dve.tensor_scalar(bias[:, :, h, :], c["ones"][:, 0:32].rearrange("p (x y) -> p x y", x=2),
                                            c["rowb"][:, 2 * HD + h:2 * HD + h + 1], None, ALU.mult)
                ins.then_inc(pre["step"], 1)
                dve.wait_ge(pre["step"], 1)
                dve.wait_ge(pre["z"], 1)
                for x in range(2):
                    cols = slice(x * 16, x * 16 + 16)
                    dve.scalar_tensor_tensor(out=zn[:, :, cols], in0=sbank[0][0:SAMPLES, 0:NC_].rearrange(
                        "p (h t) -> p h t", h=HEADS)[:, :, cols], scalar=SCALE, in1=bias[0:SAMPLES, 0, :, :],
                        op0=ALU.mult, op1=ALU.add).then_inc(pre["step"], 1)
                dve.wait_ge(pre["step"], 3)
                dve.scalar_tensor_tensor(out=xn[:, :, :], in0=zn[:, :, :], scalar=-1.0, in1=zn[:, :, :],
                                         op0=ALU.mult, op1=ALU.min).then_inc(pre["step"], 1)
                dve.wait_ge(pre["l"], 1)
                dve.scalar_tensor_tensor(out=xn[:, :, :], in0=zn[:, :, :], scalar=0.0, in1=xn[:, :, :],
                                         op0=ALU.max, op1=ALU.add).then_inc(pre["step"], 1)
                dve.wait_ge(pre["step"], 5)
                dve.wait_ge(pre["zero"], 2)
                for h in range(HEADS):
                    dve.tensor_tensor(nsp[0:SAMPLES, h, :], xn[:, h, :], c["keep_new"][:, :], ALU.mult
                                      ).then_inc(pre["step"], 1)
                dve.wait_ge(pre["z"], 2)
                dve.tensor_tensor(an[:, :, :], zn[:, :, :], sbank[1][0:SAMPLES, 0:NC_].rearrange(
                    "p (h t) -> p h t", h=HEADS), ALU.subtract).then_inc(pre["t"], 1)
                dve.wait_ge(pre["t"], 1)
                for h in range(HEADS):
                    dve.tensor_tensor(an[:, h, :], an[:, h, :], c["neg_new"][:, :], ALU.add).then_inc(pre["t"], 1)
                dve.wait_ge(pre["z"], 3)
                dve.tensor_copy(onew[:, :, :], rbank[0][:, 0:NC_].rearrange("p (h t) -> p h t", h=HEADS)
                                ).then_inc(pre["t"], 1)

        with nc.Block() as block:
            @block.sync
            def _(sp):
                with sp.Fori(0, ITERS) as i:
                    for bb in range(BI):
                        for u in range(8):
                            g, half = u // 2, u % 2
                            for x in range(PG):
                                page = sp.value_load(pages[0:1, bass.ds(i * (BI * PAGES) + (bb * PAGES + PG * g + x), 1)],
                                                     min_val=0, max_val=A["cache_sb_k"].shape[1] - 1)
                                if x == 0:
                                    wait(sp, i, "ktr", 8 * bb + u - 1)
                                src = A["cache_sb_k"][0, bass.ds(page, 1)].rearrange("o s h d -> (o s) (h d)")
                                sp.dma_start(kraw[u % 2][x * Q:(x + 1) * Q, :, :],
                                             src[:, half * HH * HD:(half + 1) * HH * HD].rearrange("(c j) n -> j c n", j=Q)
                                             ).then_inc(kl[u % 2], 16)
                        for v in range(PAGES):
                            page = sp.value_load(pages[0:1, bass.ds(i * (BI * PAGES) + (bb * PAGES + v), 1)],
                                                 min_val=0, max_val=A["cache_sb_v"].shape[1] - 1)
                            wait(sp, i, "vdone", PAGES * bb + v - 3)
                            sp.dma_start(vpage[v % 4][:, :], A["cache_sb_v"][0, bass.ds(page, 1)].rearrange(
                                "o s h d -> (o s) (h d)")).then_inc(vl[v % 4], 16)

            @block.gpsimd
            def _(gp):
                view = lambda t: t[:, :].rearrange("p (g h x t) -> p g h x t", g=PAGES // PG, h=HEADS, x=PG)

                def sums_behind(i, bb):
                    wait(gp, i, "dspr", bb + 1)
                    gp.nop().then_inc(s["passed"], 1)
                    n = PAGES * bb
                    gp.tensor_copy(view(dr)[:, 3, :, 3, :], nsp[:, :, bass.ds(i * (BI * T_S) + bb * T_S, T_S)]
                                   ).then_inc(s["rs"], 1)
                    for p in range(PAGES - 2, -1, -1):
                        n += 1
                        wait(gp, i, "rs", n)
                        g, x, g1, x1 = p // PG, p % PG, (p + 1) // PG, (p + 1) % PG
                        gp.tensor_tensor(view(dr)[:, g, :, x, :], view(dr)[:, g1, :, x1, :], view(dsp)[:, g1, :, x1, :],
                                         ALU.add).then_inc(s["rs"], 1)
                    wait(gp, i, "rs", n + 1)
                    gp.nop().then_inc(s["rr"], 1)

                def queries(i, bb):
                    wait(gp, i, "kr", 8 * bb)
                    for half in range(2):
                        pitch = PG * UR + PG * T_S
                        place = qd[:, half * HH * PG * UR:][:, 0:HH * pitch].rearrange("p (h w) -> p h w", w=pitch)
                        place = place[:, :, 0:PG * UR].rearrange("p h (f c) -> p h f c", c=UR)
                        for x in range(PG):
                            r = slice(x * Q, (x + 1) * Q)
                            gp.nop().then_inc(s["passed"], 1)
                            src = qs[r, half * HH * PG:(half + 1) * HH * PG, bass.ds(i * (BI * T_S) + bb * T_S, T_S)]
                            gp.tensor_copy(place[r, :, :, x * T_S:(x + 1) * T_S],
                                           src.rearrange("p (h f) t -> p h f t", f=PG)).then_inc(s["qb"], 1)
                            wait(gp, i, "qb", 2 * PG * bb + PG * half + x + 1)

                one = lambda t, i, hh: t[bass.ds(i * HI + hh, 1), :, 0:SEQ].rearrange("o p t -> (o p) t")

                def load(i, hh):
                    gp.dma_start(kh[:, hh, :], one(S["kT"], i, hh)).then_inc(hl[hh], 16)
                    gp.dma_start(qh[:, hh, :], one(S["qT"], i, hh)).then_inc(hl[hh], 16)
                    gp.dma_start(vh[:, hh, :, :], O["sbv_p"][0, 0, :, bass.ds(i * HI + hh, 1), :].rearrange(
                        "(t p) o d -> p t (o d)", p=P)).then_inc(hl[hh], 16)

                def finish(i, hh, more):
                    wait(gp, i, "oev", 2 * hh + 2)
                    gp.nop().then_inc(s["passed"], 1)
                    gp.dma_start(one(S["yT1"], i, hh), gh[:, hh, :]).then_inc(ys[hh], 16)
                    if more:
                        load(i + 1, hh)
                        gp.wait_ge(ys[hh], i * 16 + 16)
                        gp.nop().then_inc(s["passed"], 1)
                        gp.dma_start(gh[:, hh, :], one(S["gT"], i + 1, hh)).then_inc(hl[hh], 16)

                def iteration(i, more):
                    sums_behind(i, 0)
                    queries(i, 1)
                    finish(i, 0, more)
                    finish(i, 1, more)
                    sums_behind(i, 1)
                    if more:
                        queries(i + 1, 0)
                    finish(i, 2, more)
                queries(0, 0)
                for hh in range(HI):
                    load(0, hh)
                    gp.dma_start(gh[:, hh, :], one(S["gT"], 0, hh)).then_inc(hl[hh], 16)
                with gp.Fori(0, ITERS - 1) as i:
                    iteration(i, True)
                iteration(ITERS - 1, False)
                for hh in range(HI):
                    gp.wait_ge(ys[hh], 16 * ITERS)

            @block.scalar
            def _(act):
                def evacuate(i, t):
                    hh, ch, kb, q0, n, diag, first, last = steps[t]
                    wait(act, i, "zr", t + 1)
                    wait(act, i, "tsub", t - 2)
                    act.activation(z[:, t % 3, 0:n], zbank[t % 2][:, 0:n], ACT.Identity,
                                   bias=bcol[:, hh:hh + 1], scale=SCALE).then_inc(s["zev"], 1)

                def log_part(i, t):
                    n = steps[t][4]
                    wait(act, i, "nab", t + 1)
                    act.activation(soft[:, t % 2, 0:n], soft[:, t % 2, 0:n], ACT.Exp).then_inc(s["ee"], 1)
                    wait(act, i, "ee", t + 1)
                    act.activation(soft[:, t % 2, 0:n], soft[:, t % 2, 0:n], ACT.Ln, bias=1.0).then_inc(s["el"], 1)

                def step(i, t):
                    if t + 2 < NSTEP:
                        evacuate(i, t + 2)
                    if t + 1 < NSTEP:
                        log_part(i, t + 1)
                    n = steps[t][4]
                    wait(act, i, "tsub", t + 1)
                    act.activation(a[:, t % 3, 0:n], a[:, t % 3, 0:n], ACT.Exp).then_inc(s["ax"], 1)

                def rows_out(i, bb, u):
                    wait(act, i, "kr", 8 * bb + u + 1)
                    wait(act, i, "kdone", 8 * bb + u - 1)
                    act.activation(kev[:, u % 2, :], rbank[u % 2][0:UR, 0:P], ACT.Copy).then_inc(s["rev"], 1)

                def weights(i, bb):
                    wait(act, i, "dt", 2 * bb + 2)
                    wait(act, i, "vdone", PAGES * bb)
                    for g in range(PAGES // PG):
                        act.activation(daw[:, PG * g:PG * (g + 1), :].rearrange("p x (h t) -> p x h t", t=T_S),
                                       da[:, g * GC:(g + 1) * GC].rearrange("p (h x t) -> p x h t", h=HEADS, x=PG),
                                       ACT.Exp).then_inc(s["dax"], 1)

                def values_out(i, bb):
                    wait(act, i, "vdone", PAGES * (bb + 1))
                    wait(act, i, "sel", bb)
                    for n in (2, 0, 1):
                        act.activation(vev[:, n * VC:(n + 1) * VC], (sbank[0], sbank[1], rbank[0])[n][0:HEADS * T_S, :],
                                       ACT.Copy).then_inc(s["ve"], 1)
                act.preload_act_table_set("natural_log_exp_and_others")
                for name in ("zev", "rev", "ve", "dax"):
                    act.nop().then_inc(s[name], ahead[name])
                with act.Fori(0, ITERS) as i:
                    wait(act, i, "bc", 1)
                    evacuate(i, 0)
                    evacuate(i, 1)
                    log_part(i, 0)
                    for e in order:
                        if e[0] == "P":
                            step(i, e[1])
                            r, bb = e[1] % (NSTEP // BI), e[1] // (NSTEP // BI)
                            if r == 8:
                                wait(act, i, "dnab", bb + 1)
                                act.activation(dx[:, :], dx[:, :], ACT.Exp).then_inc(s["dee"], 1)
                                wait(act, i, "dee", bb + 1)
                                act.activation(dx[:, :], dx[:, :], ACT.Ln, bias=1.0).then_inc(s["dl"], 1)
                            if r == 10:
                                weights(i, bb)
                        if e[0] == "K":
                            rows_out(i, e[1], e[2])
                        if e[0] == "V" and e[2] == PAGES - 1:
                            values_out(i, e[1])

            @block.vector
            def _(dve):
                def negated(i, t):
                    n = steps[t][4]
                    wait(dve, i, "zev", t + 1)
                    dve.scalar_tensor_tensor(out=soft[:, t % 2, 0:n], in0=z[:, t % 3, 0:n], scalar=-1.0,
                                             in1=z[:, t % 3, 0:n], op0=ALU.mult, op1=ALU.min).then_inc(s["nab"], 1)

                def diagonals(t):
                    return sum(x[5] for x in steps[:t])

                def softplus(i, t):
                    n, diag = steps[t][4:6]
                    wait(dve, i, "el", t + 1)
                    wait(dve, i, "pvd", t - 2)
                    dve.scalar_tensor_tensor(out=spl[:, t % 3, 0:n], in0=z[:, t % 3, 0:n], scalar=0.0,
                                             in1=soft[:, t % 2, 0:n], op0=ALU.max, op1=ALU.add
                                             ).then_inc(s["spm" if diag else "spr"], 1)
                    if diag:
                        wait(dve, i, "spm", diagonals(t) + 1)
                        dve.tensor_tensor(spl[:, t % 3, 0:P], spl[:, t % 3, 0:P], c["keep"][:, :], ALU.mult
                                          ).then_inc(s["spr"], 1)

                def exponent(i, t):
                    n, diag = steps[t][4:6]
                    lo = 512 - n
                    wait(dve, i, "tri", t + 1)
                    wait(dve, i, "pvd", t - 2)
                    dve.tensor_tensor(a[:, t % 3, 0:n], z[:, t % 3, 0:n], cbank[:, lo:512], ALU.subtract
                                      ).then_inc(s["tm" if diag else "tsub"], 1)
                    if diag:
                        wait(dve, i, "tm", diagonals(t) + 1)
                        dve.tensor_tensor(a[:, t % 3, 0:P], a[:, t % 3, 0:P], c["neg"][:, :], ALU.add
                                          ).then_inc(s["tsub"], 1)

                def output(i, t):
                    hh, ch = steps[t][0:2]
                    wait(dve, i, "pvd", t + 1)
                    cols = slice(ch * 512, (ch + 1) * 512)
                    dve.tensor_tensor(gh[:, hh, cols], obank[:, :], gh[:, hh, cols], ALU.mult).then_inc(s["oev"], 1)

                def step(i, t):
                    if t + 2 < NSTEP:
                        negated(i, t + 2)
                    if t + 1 < NSTEP:
                        softplus(i, t + 1)
                    exponent(i, t)
                    if t and steps[t - 1][7]:
                        output(i, t - 1)

                def turn(i, bb, u):
                    dve.wait_ge(kl[u % 2], i * (BI * 4 * 64) + (bb * 4 + u // 2 + 1) * 64)
                    wait(dve, i, "kr", 8 * bb + u - 1)
                    dve.transpose(kt[u % 2][:, :, :, :].rearrange("p h f (c j) -> p c (h f) j", j=Q),
                                  kraw[u % 2][:, :, :].rearrange("p c (f j) -> p c f j", j=Q)).then_inc(s["ktr"], 1)

                def sample_scores(i, bb):
                    for x in range(2):
                        wait(dve, i, "kdone", 8 * bb + 4 * x + 4)
                        cols = slice(2 * x * GC, 2 * (x + 1) * GC)
                        dve.scalar_tensor_tensor(out=dz[:, cols], in0=sbank[x][:, 0:2 * GC], scalar=SCALE,
                                                 in1=bias[:, :, :, :].rearrange("p g h t -> p (g h t)"), op0=ALU.mult,
                                                 op1=ALU.add).then_inc(s["dzev"], 1)
                    wait(dve, i, "dzev", 2 * bb + 2)
                    dve.scalar_tensor_tensor(out=dx[:, :], in0=dz[:, :], scalar=-1.0, in1=dz[:, :], op0=ALU.mult,
                                             op1=ALU.min).then_inc(s["dnab"], 1)

                def sample_softplus(i, bb):
                    wait(dve, i, "dl", bb + 1)
                    dve.scalar_tensor_tensor(out=dsp[:, :], in0=dz[:, :], scalar=0.0, in1=dx[:, :], op0=ALU.max,
                                             op1=ALU.add).then_inc(s["dspr"], 1)

                def sample_exponent(i, bb):
                    wait(dve, i, "dax", 4 * bb)
                    for x in range(2):
                        wait(dve, i, "dc", 2 * bb + x + 1)
                        cols = slice(2 * x * GC, 2 * (x + 1) * GC)
                        dve.tensor_tensor(da[:, cols], dz[:, cols], sbank[x][:, 0:2 * GC], ALU.subtract
                                          ).then_inc(s["dt"], 1)
                def sample_output(i, bb):
                    wait(dve, i, "sel", bb + 1)
                    cols = bass.ds(i * (BI * T_S) + bb * T_S, T_S)
                    dve.tensor_tensor(onew[:, :, cols], rbank[1][:, 0:HEADS * T_S].rearrange("p (h t) -> p h t", h=HEADS),
                                      onew[:, :, cols], ALU.add).then_inc(s["so"], 1)
                for name in ("tsub", "oev", "ktr", "so"):
                    dve.nop().then_inc(s[name], ahead[name])
                with dve.Fori(0, ITERS) as i:
                    dve.tensor_copy(bcol[:, :], c["rowb"][:, bass.ds(i * HI + 2 * HD, HI)]).then_inc(s["bc"], 1)
                    turn(i, 0, 0)
                    negated(i, 0)
                    negated(i, 1)
                    softplus(i, 0)
                    for e in order:
                        if e[0] == "K" and e[2] < 7:
                            turn(i, e[1], e[2] + 1)
                        if e[0] == "S":
                            sample_output(i, e[1])
                        if e == ("V", 0, PAGES - 2):
                            turn(i, 1, 0)
                        if e[0] == "C":
                            sample_exponent(i, e[1])
                        if e[0] == "P":
                            r, bb = e[1] % (NSTEP // BI), e[1] // (NSTEP // BI)
                            if r == 8:
                                sample_scores(i, bb)
                            step(i, e[1])
                            if r == 8:
                                sample_softplus(i, bb)
                    output(i, NSTEP - 1)
                    sample_output(i, 1)
                wait(dve, ITERS, "so", 0)
                dve.tensor_tensor(gs[:, :, :], onew[:, :, :], gs[:, :, :], ALU.mult).then_inc(s["pre"], 1)

            @block.tensor
            def _(pe):
                def scores(i, t):
                    hh, ch, kb, q0, n, diag, first, last = steps[t]
                    wait(pe, i, "zev", t - 1)
                    if first and ch == 0:
                        pe.wait_ge(hl[hh], i * 64 + 64)
                    pe.matmul(zbank[t % 2][:, 0:n], kh[:, hh, kb * P:(kb + 1) * P], qh[:, hh, q0:q0 + n], start=True,
                              stop=True).then_inc(s["zr"], 1)

                def values(i, t):
                    hh, ch, kb, q0, n, diag, first, last = steps[t]
                    wait(pe, i, "ax", t + 1)
                    if first:
                        wait(pe, i, "oev", 2 * hh + ch)
                    pe.matmul(obank[:, 512 - n:512], vh[:, hh, kb, :], a[:, t % 3, 0:n], start=first, stop=last,
                              skip_group_check=True).then_inc(s["pvd"], 1)

                def step(i, t):
                    if t + 2 < NSTEP:
                        scores(i, t + 2)
                    wait(pe, i, "tsub", t)
                    n, first, last = steps[t][4], steps[t][6], steps[t][7]
                    if t and not steps[t - 1][7]:
                        m = steps[t - 1][4]
                        pe.matmul(cbank[:, 512 - m:512], c["before"][:, :], spl[:, (t - 1) % 3, 0:m], start=False,
                                  stop=False, skip_group_check=True)
                    wait(pe, i, "spr", t + 1)
                    pe.matmul(cbank[:, 512 - n:512], c["suffix"][:, :], spl[:, t % 3, 0:n], start=first, stop=False,
                              skip_group_check=True).then_inc(s["tri"], 1)
                    if t:
                        values(i, t - 1)

                def unit(i, bb, u):
                    wait(pe, i, "ktr", 8 * bb + u + 1)
                    wait(pe, i, "qb", 2 * PG * (bb + 1))
                    wait(pe, i, "rev", 8 * bb + u - 1)
                    if u == 0:
                        wait(pe, i, "ve", 3 * bb - 2)
                    if u == 1:
                        wait(pe, i, "so", bb)
                    for h in range(HH):
                        for f in range(PG):
                            at = (((u % 2) * HH + h) * PG + f) * UR
                            ins = pe.matmul(rbank[u % 2][0:UR, 0:P], qd[:, at:at + UR], kt[u % 2][:, h, f, :],
                                            start=h == 0 and f == 0, stop=h == HH - 1 and f == PG - 1)
                    ins.then_inc(s["kr"], 1)

                def turned(i, bb, u):
                    wait(pe, i, "rev", 8 * bb + u + 1)
                    if u == 0:
                        wait(pe, i, "ve", 3 * bb)
                    at = (u // 2 % 2) * GC + (u % 2) * UR
                    pe.transpose(sbank[u // 4][:, at:at + UR], kev[:, u % 2, :], c["ident"][0:UR, 0:UR]
                                 ).then_inc(s["kdone"], 1)

                def sums(i, bb, _):
                    wait(pe, i, "dzev", 2 * bb + 2)
                    wait(pe, i, "dspr", bb + 1)
                    wait(pe, i, "rr", bb + 1)
                    for x in range(2):
                        cols = slice(2 * x * GC, 2 * (x + 1) * GC)
                        pe.matmul(sbank[x][:, 0:2 * GC], c["suffix"][:, :], dsp[:, cols], start=True, stop=False)
                        pe.matmul(sbank[x][:, 0:2 * GC], c["ones"][:, :], dr[:, cols], start=False, stop=True
                                  ).then_inc(s["dc"], 1)

                def page(i, bb, v):
                    pe.wait_ge(vl[v % 4], i * (BI * 4 * 16) + (bb * 4 + v // 4 + 1) * 16)
                    if v == 0:
                        wait(pe, i, "dax", 4 * (bb + 1))
                        wait(pe, i, "dt", 2 * (bb + 1))
                        wait(pe, i, "rev", 8 * (bb + 1))
                    for n in range(3):
                        ins = pe.matmul((sbank[0], sbank[1], rbank[0])[n][0:HEADS * T_S, :], daw[:, v, :],
                                        vpage[v % 4][:, n * VC:(n + 1) * VC], start=v == 0, stop=v == PAGES - 1)
                    ins.then_inc(s["vdone"], 1)

                def select(i, bb, _):
                    wait(pe, i, "ve", 3 * (bb + 1))
                    wait(pe, i, "rev", 8 * (bb + 1))
                    wait(pe, i, "so", bb)
                    for h in range(HEADS):
                        own = slice(h * T_S, (h + 1) * T_S)
                        ins = pe.matmul(rbank[1][:, own], vev[:, h * HD:(h + 1) * HD], c["ident"][0:HEADS * T_S, own],
                                        start=True, stop=True)
                    ins.then_inc(s["sel"], 1)
                for name in ("pvd", "kdone", "kr", "vdone", "sel"):
                    pe.nop().then_inc(s[name], ahead[name])
                with pe.Fori(0, ITERS) as i:
                    scores(i, 0)
                    scores(i, 1)
                    for e in order:
                        if e[0] == "P":
                            step(i, e[1])
                        else:
                            {"K": unit, "T": turned, "C": sums, "V": page, "S": select}[e[0]](i, e[1], e[2])
                    values(i, NSTEP - 1)
                    select(i, 1, 0)

        with nc.Block() as block:
            @block.sync
            def _(sp):
                for h in range(HEADS):
                    sp.dma_start(S["yT1"][h, :, SEQ:T], gs[:, h, :]).then_inc(s["ys_end"], 16)
                sp.wait_ge(s["ys_end"], 16 * HEADS)


def program(nc, A, O):
    S = {n: nc.dram_tensor(f"scratch_{n}", shape, F32, kind="Internal").ap() for n, shape in (
        ("yT0", (16, P, T)), ("yT1", (16, P, T)), ("x1", (T, D)), ("qT", (HEADS, P, T)), ("kT", (HEADS, P, T)),
        ("gT", (HEADS, P, T)))}
    with ExitStack() as ctx:
        k = Kit(nc, ctx, "c_")
        c = {"ident": k.sb("ident", [P, P]), "ones": k.sb("ones", [P, P]), "suffix": k.sb("suffix", [P, P]),
             "before": k.sb("before", [P, P]), "neg": k.sb("neg", [P, P]), "keep": k.sb("keep", [P, P]),
             "keep_new": k.sb("keep_new", [SAMPLES, SAMPLES]), "neg_new": k.sb("neg_new", [SAMPLES, SAMPLES]),
             "short": k.sb("short", [P, GROUPS, 16]), "vec": k.sb("vec", [P, 46]),
             "rowb": k.sb("rowb", [P, 2 * HD + HEADS])}
        setup_phase(nc, c, A)

        def x_rows(t):
            if t < TILES:
                return [(0, P, A["x_prompt"][0, t * P:(t + 1) * P, :])]
            return [(0, P - SAMPLES, A["x_prompt"][0, LAST:SEQ, :]),
                    (P - SAMPLES, P, A["x_sample"].rearrange("b t d -> (b t) d"))]

        def x1_rows(t):
            return [(0, P, S["x1"][t * P:(t + 1) * P, :])] if t < TILES else [(0, P, S["x1"][LAST:T, :])]

        def x1_out(t):
            return (0, P, S["x1"][t * P:(t + 1) * P, :]) if t < TILES else (P - SAMPLES, P, S["x1"][SEQ:T, :])

        def y_out(t):
            return ((0, P, O["y_prompt"][0, t * P:(t + 1) * P, :]) if t < TILES else
                    (P - SAMPLES, P, O["y_sample"].rearrange("b t d -> (b t) d")))

        for i in range(2):
            with ExitStack() as hctx:
                kh = Kit(nc, hctx, f"h{i}_")
                hT_hi = kh.sb("hT_hi", [P, KD, T], F32R)
                hT_lo = kh.sb("hT_lo", [P, KD, T], F32R)
                norm_phase(nc, c, hT_hi, hT_lo, (x_rows, x1_rows)[i], 8 * i)
                if i == 0:
                    pool_phase(nc, c, A, O, {"yT": S["yT0"]}, hT_hi, hT_lo)
                    w_in, q0 = A["w_in_pool"][0], 2 * BW
                else:
                    in_phase(nc, c, A, O, S, hT_hi, hT_lo)
                    w_in, q0 = A["w_in_sb"][0], 4 * BW
                with ExitStack() as mctx:
                    km = Kit(nc, mctx, f"mem{i}_")
                    c["mkT"], c["mv"] = km.sb("mkT", [P, MH, MEM]), km.sb("mv", [P, MJ, MW])
                    memory_kv_phase(nc, c, A, O, i)
                    memory_attention_phase(nc, c, A, S[f"yT{i}"], i, w_in, q0, q0 + MW, hT_hi, hT_lo)
            if i:
                stick_phase(nc, c, A, O, S)
            out_phase(nc, c, A, S[f"yT{i}"], i, (x_rows, x1_rows)[i], (x1_out, y_out)[i])


_INS = ["x_prompt", "x_sample", "cache_mem_k", "cache_mem_v", "state_pool", "cache_sb_k", "cache_sb_v", "page_table",
        "mem_prompt", "norm_g", "w_in_pool", "w_pool_grp", "pool_scale", "w_in_sb", "sb_bias", "mem_norm_g", "w_mem_kv",
        "mem_q_g", "mem_k_g", "w_out"]
_OUTS = [("y_prompt", (1, SEQ, D)), ("y_sample", (NB_S, T_S, D)),
         ("mem_k", (2, 1, MEM, MH, HD)), ("mem_v", (2, 1, MEM, MH, HD)),
         ("pool_p", (1, 1, HIST, BW)), ("pool_s", (1, NB_S, HIST, BW)),
         ("sbk_p", (1, 1, SEQ, HEADS, HD)), ("sbv_p", (1, 1, SEQ, HEADS, HD)),
         ("sbk_s", (1, NB_S, T_S, HEADS, HD)), ("sbv_s", (1, NB_S, T_S, HEADS, HD))]


def kernel(**inputs):
    import numpy as _np
    import concourse.bacc as _bacc
    from concourse import mybir as _mybir
    from concourse.bass_utils import run_bass_kernel_spmd as _run

    nc = _bacc.Bacc("TRN2", target_bir_lowering=False, num_devices=1)
    arrays, A, O = {}, {}, {}
    for name in _INS:
        a = _np.ascontiguousarray(inputs[name])
        arrays[f"in_{name}_dram"] = a
        A[name] = nc.dram_tensor(f"in_{name}_dram", a.shape, _mybir.dt.from_np(a.dtype), kind="ExternalInput").ap()
    for name, shape in _OUTS:
        O[name] = nc.dram_tensor(f"out_{name}_dram", shape, _mybir.dt.float32, kind="ExternalOutput").ap()
    program(nc, A, O)
    r = _run(nc, [arrays], core_ids=[0])
    return tuple(r.results[0][f"out_{name}_dram"] for name, _ in _OUTS)
```
